# Optimizing a Trainium2 kernel written in Bass

```python
import jax, jax.numpy as jnp
from jax import lax
import numpy as np
import math

D_MODEL = 2048
BATCH = 1
SEQ = 256
DEPTH = 1

N_MIXERS = 3
GRID_W = 64
BRANCH_W = D_MODEL
NORM_EPS = 1e-6

POOL_WINDOWS = (2, 4, 8, 16)
N_POOL_GROUPS = 4
POOL_GROUP_DIM = BRANCH_W // N_POOL_GROUPS

GLA_HEADS = 4
GLA_KEY_W = D_MODEL // 2
GLA_VAL_W = BRANCH_W
GLA_DK = GLA_KEY_W // GLA_HEADS
GLA_DV = GLA_VAL_W // GLA_HEADS
GLA_LOWRANK = 16
GLA_TAU = 16.0
GLA_CHUNK = 64

ATTN_HEAD_DIM = 128
ATTN_HEADS = BRANCH_W // ATTN_HEAD_DIM
ATTN_KV_HEADS = 4
ATTN_GROUP = ATTN_HEADS // ATTN_KV_HEADS
ATTN_Q_W = ATTN_HEADS * ATTN_HEAD_DIM
ATTN_KV_W = ATTN_KV_HEADS * ATTN_HEAD_DIM
ATTN_BLOCK = 128
ROPE_AXIS_DIM = ATTN_HEAD_DIM // 2
ROPE_THETA = 10000.0


def rms_norm(x, eps=NORM_EPS):
    xf = x.astype(jnp.float32)
    return (xf * lax.rsqrt(jnp.mean(xf * xf, axis=-1, keepdims=True) + eps)).astype(x.dtype)

def ada_modulation(c, w, b):
    m = jnp.dot(jax.nn.silu(c), w) + b
    shift, scale, gate = jnp.split(m, 3, axis=-1)
    return shift[:, None], scale[:, None], gate[:, None]

def centred_window_mean(u, w):
    T = u.shape[1]
    csum = jnp.cumsum(u.astype(jnp.float32), axis=1)
    P = jnp.concatenate([jnp.zeros_like(csum[:, :1]), csum], axis=1)
    t = jnp.arange(T)
    lo = jnp.maximum(t - w // 2, 0)
    hi = jnp.minimum(t + w // 2, T)
    cnt = (hi - lo).astype(jnp.float32)
    return ((P[:, hi] - P[:, lo]) / cnt[None, :, None]).astype(u.dtype)

def pool_mixer(h, w_in, w_grp, scale, w_out):
    B, T, _ = h.shape
    u, g = jnp.split(h @ w_in, 2, axis=-1)
    ug = u.reshape(B, T, N_POOL_GROUPS, POOL_GROUP_DIM)
    pooled = jnp.stack(
        [centred_window_mean(ug[:, :, i], w) - ug[:, :, i] for i, w in enumerate(POOL_WINDOWS)],
        axis=2)
    y = jnp.einsum('btgc,gcd->btgd', pooled, w_grp).reshape(B, T, BRANCH_W) * scale
    return (y * jax.nn.silu(g)) @ w_out

def gla_chunked_scan(q, k, v, log_a, include_diag):
    B, T, H, DK = q.shape
    DV = v.shape[-1]
    nc = T // GLA_CHUNK

    def to_chunks(z):
        return z.astype(jnp.float32).reshape(B, nc, GLA_CHUNK, H, z.shape[-1]).transpose(1, 0, 3, 2, 4)

    qc, kc, vc, ac = to_chunks(q), to_chunks(k), to_chunks(v), to_chunks(log_a)
    mask = jnp.tril(jnp.ones((GLA_CHUNK, GLA_CHUNK), dtype=bool), 0 if include_diag else -1)

    def step(S, inp):
        qi, ki, vi, ai = inp
        b = jnp.cumsum(ai, axis=2)
        o_inter = jnp.einsum('bhcd,bhde->bhce', qi * jnp.exp(b), S)
        diff = b[:, :, :, None, :] - b[:, :, None, :, :]
        decay = jnp.exp(jnp.where(mask[:, :, None], diff, -jnp.inf))
        A = jnp.sum(qi[:, :, :, None, :] * ki[:, :, None, :, :] * decay, axis=-1)
        o_intra = jnp.einsum('bhij,bhje->bhie', A, vi)
        b_last = b[:, :, -1:, :]
        S_new = jnp.exp(b_last[:, :, 0, :])[..., None] * S + jnp.einsum(
            'bhjd,bhje->bhde', ki * jnp.exp(b_last - b), vi)
        return S_new, o_inter + o_intra

    S0 = jnp.zeros((B, H, DK, DV), jnp.float32)
    _, o = lax.scan(step, S0, (qc, kc, vc, ac))
    return o.transpose(1, 0, 3, 2, 4).reshape(B, T, H, DV)

def gla_mixer(h, w_in, fwd_w1, fwd_w2, fwd_b, bwd_w1, bwd_w2, bwd_b, norm_g, w_out):
    B, T, _ = h.shape
    q, k, v, g = jnp.split(h @ w_in, [GLA_KEY_W, 2 * GLA_KEY_W, 2 * GLA_KEY_W + GLA_VAL_W], axis=-1)
    q = (q * GLA_DK ** -0.5).reshape(B, T, GLA_HEADS, GLA_DK)
    k = k.reshape(B, T, GLA_HEADS, GLA_DK)
    v = v.reshape(B, T, GLA_HEADS, GLA_DV)

    def log_decay(w1, w2, b):
        z = ((h @ w1) @ w2 + b).astype(jnp.float32)
        return (jax.nn.log_sigmoid(z) / GLA_TAU).reshape(B, T, GLA_HEADS, GLA_DK)

    rev = lambda z: z[:, ::-1]
    o_fwd = gla_chunked_scan(q, k, v, log_decay(fwd_w1, fwd_w2, fwd_b), include_diag=True)
    o_bwd = rev(gla_chunked_scan(rev(q), rev(k), rev(v), rev(log_decay(bwd_w1, bwd_w2, bwd_b)),
                                 include_diag=False))
    o = (rms_norm(o_fwd + o_bwd) * norm_g).reshape(B, T, GLA_VAL_W).astype(h.dtype)
    return (o * jax.nn.silu(g)) @ w_out

def axial_rope_tables(T):
    rows = T // GRID_W
    t = jnp.arange(T)
    row = (t // GRID_W - rows // 2).astype(jnp.float32)
    col = (t % GRID_W - GRID_W // 2).astype(jnp.float32)
    inv = ROPE_THETA ** (-jnp.arange(0, ROPE_AXIS_DIM, 2, dtype=jnp.float32) / ROPE_AXIS_DIM)
    ang = jnp.concatenate([row[:, None] * inv, col[:, None] * inv], axis=-1)
    return jnp.cos(ang), jnp.sin(ang)

def apply_rope(x, cos, sin):
    shp = (cos.shape[0],) + (1,) * (x.ndim - 3) + (cos.shape[1],)
    cos = cos.reshape(shp).astype(x.dtype)
    sin = sin.reshape(shp).astype(x.dtype)
    xr = x.reshape(x.shape[:-1] + (-1, 2))
    x0, x1 = xr[..., 0], xr[..., 1]
    return jnp.stack([x0 * cos - x1 * sin, x0 * sin + x1 * cos], axis=-1).reshape(x.shape)

def attn_mixer(h, w_in, q_norm_g, k_norm_g, w_out):
    B, T, _ = h.shape
    q, k, v, g = jnp.split(h @ w_in, [ATTN_Q_W, ATTN_Q_W + ATTN_KV_W, ATTN_Q_W + 2 * ATTN_KV_W], axis=-1)
    q = rms_norm(q.reshape(B, T, ATTN_KV_HEADS, ATTN_GROUP, ATTN_HEAD_DIM)) * q_norm_g
    k = rms_norm(k.reshape(B, T, ATTN_KV_HEADS, ATTN_HEAD_DIM)) * k_norm_g
    v = v.reshape(B, T, ATTN_KV_HEADS, ATTN_HEAD_DIM)
    cos, sin = axial_rope_tables(T)
    q = apply_rope(q, cos, sin) * ATTN_HEAD_DIM ** -0.5
    k = apply_rope(k, cos, sin)
    nb = T // ATTN_BLOCK
    qb = q.reshape(B, nb, ATTN_BLOCK, ATTN_KV_HEADS, ATTN_GROUP, ATTN_HEAD_DIM).transpose(1, 0, 2, 3, 4, 5)

    def block(qi):
        s = jnp.einsum('bqkgd,bskd->bkgqs', qi, k, preferred_element_type=jnp.float32)
        p = jax.nn.softmax(s, axis=-1).astype(v.dtype)
        return jnp.einsum('bkgqs,bskd->bqkgd', p, v)

    o = lax.map(block, qb).transpose(1, 0, 2, 3, 4, 5).reshape(B, T, ATTN_Q_W)
    return (o * jax.nn.silu(g)) @ w_out

def first_inputs(seed: int = 0) -> dict:
    key = jax.random.key(seed)
    ks = iter(jax.random.split(key, 40))
    n_pool = len(range(0, DEPTH, N_MIXERS))
    n_gla = len(range(1, DEPTH, N_MIXERS))
    n_attn = len(range(2, DEPTH, N_MIXERS))
    D = D_MODEL

    def nrm(shape, scale):
        return jax.random.normal(next(ks), shape, jnp.float32) * scale

    def gain(shape):
        return 1.0 + 0.1 * jax.random.normal(next(ks), shape, jnp.float32)

    return {
        "x": nrm((BATCH, SEQ, D), 1.0),
        "c": nrm((BATCH, D), 1.0),
        "w_mod": nrm((DEPTH, D, 3 * D), 0.5 * D ** -0.5),
        "b_mod": nrm((DEPTH, 3 * D), 0.02),
        "pool_w_in": nrm((n_pool, D, 2 * BRANCH_W), D ** -0.5),
        "pool_w_grp": nrm((n_pool, N_POOL_GROUPS, POOL_GROUP_DIM, POOL_GROUP_DIM), POOL_GROUP_DIM ** -0.5),
        "pool_scale": gain((n_pool, BRANCH_W)),
        "pool_w_out": nrm((n_pool, BRANCH_W, D), BRANCH_W ** -0.5),
        "gla_w_in": nrm((n_gla, D, 2 * GLA_KEY_W + 2 * GLA_VAL_W), D ** -0.5),
        "gla_fwd_w1": nrm((n_gla, D, GLA_LOWRANK), D ** -0.5),
        "gla_fwd_w2": nrm((n_gla, GLA_LOWRANK, GLA_KEY_W), GLA_LOWRANK ** -0.5),
        "gla_fwd_b": nrm((n_gla, GLA_KEY_W), 0.1),
        "gla_bwd_w1": nrm((n_gla, D, GLA_LOWRANK), D ** -0.5),
        "gla_bwd_w2": nrm((n_gla, GLA_LOWRANK, GLA_KEY_W), GLA_LOWRANK ** -0.5),
        "gla_bwd_b": nrm((n_gla, GLA_KEY_W), 0.1),
        "gla_norm_g": gain((n_gla, GLA_DV)),
        "gla_w_out": nrm((n_gla, GLA_VAL_W, D), GLA_VAL_W ** -0.5),
        "attn_w_in": nrm((n_attn, D, 2 * ATTN_Q_W + 2 * ATTN_KV_W), D ** -0.5),
        "attn_q_norm_g": gain((n_attn, ATTN_HEAD_DIM)),
        "attn_k_norm_g": gain((n_attn, ATTN_HEAD_DIM)),
        "attn_w_out": nrm((n_attn, ATTN_Q_W, D), ATTN_Q_W ** -0.5),
        "final_norm_g": gain((D,)),
    }

def first_block(x, c, w_mod, b_mod, pool_w_in, pool_w_grp, pool_scale, pool_w_out,
              gla_w_in, gla_fwd_w1, gla_fwd_w2, gla_fwd_b, gla_bwd_w1, gla_bwd_w2, gla_bwd_b,
              gla_norm_g, gla_w_out, attn_w_in, attn_q_norm_g, attn_k_norm_g, attn_w_out,
              final_norm_g):
    for i in range(DEPTH):
        shift, scale, gate = ada_modulation(c, w_mod[i], b_mod[i])
        h = rms_norm(x) * (1.0 + scale) + shift
        kind, j = i % N_MIXERS, i // N_MIXERS
        if kind == 0:
            y = pool_mixer(h, pool_w_in[j], pool_w_grp[j], pool_scale[j], pool_w_out[j])
        elif kind == 1:
            y = gla_mixer(h, gla_w_in[j], gla_fwd_w1[j], gla_fwd_w2[j], gla_fwd_b[j],
                          gla_bwd_w1[j], gla_bwd_w2[j], gla_bwd_b[j], gla_norm_g[j], gla_w_out[j])
        else:
            y = attn_mixer(h, attn_w_in[j], attn_q_norm_g[j], attn_k_norm_g[j], attn_w_out[j])
        x = x + gate * y
    return rms_norm(x) * final_norm_g


DEPTH_2 = 2

CHUNK = 64
N_MIXERS_2 = 2
EPS = 1e-6

A_HEADS = 16
A_HEAD_DIM = 128
A_INNER = A_HEADS * A_HEAD_DIM
CONV_K = 4

B_HEADS = 16
B_HEAD_DIM = 128
B_INNER = B_HEADS * B_HEAD_DIM
LEFT_CHUNKS = 8
BAND = (LEFT_CHUNKS + 1) * CHUNK
REL_CLIP = 256


def rms_norm_2(x, w):
    xf = x.astype(jnp.float32)
    y = xf * lax.rsqrt(jnp.mean(xf * xf, axis=-1, keepdims=True) + EPS)
    return (y * w.astype(jnp.float32)).astype(x.dtype)

def l2_norm(x):
    xf = x.astype(jnp.float32)
    return xf * lax.rsqrt(jnp.sum(xf * xf, axis=-1, keepdims=True) + EPS)

def causal_depthwise_conv(x, w):
    c = x.shape[-1]
    return lax.conv_general_dilated(
        x, w[:, None, :].astype(x.dtype), window_strides=(1,),
        padding=[(CONV_K - 1, 0)], dimension_numbers=("NWC", "WIO", "NWC"),
        feature_group_count=c)

def gated_deltanet(h, w_in, conv_w, a_log, dt_bias, out_norm_w, w_out):
    bsz, t, _ = h.shape
    nc = t // CHUNK
    proj = h @ w_in.astype(h.dtype)
    qkv = proj[..., :3 * A_INNER]
    z = proj[..., 3 * A_INNER:4 * A_INNER]
    a_in = proj[..., 4 * A_INNER:4 * A_INNER + A_HEADS]
    b_in = proj[..., 4 * A_INNER + A_HEADS:]
    qkv = jax.nn.silu(causal_depthwise_conv(qkv, conv_w))
    q = qkv[..., :A_INNER].reshape(bsz, t, A_HEADS, A_HEAD_DIM)
    k = qkv[..., A_INNER:2 * A_INNER].reshape(bsz, t, A_HEADS, A_HEAD_DIM)
    v = qkv[..., 2 * A_INNER:].reshape(bsz, t, A_HEADS, A_HEAD_DIM).astype(jnp.float32)
    q = l2_norm(q) * (A_HEAD_DIM ** -0.5)
    k = l2_norm(k)
    beta = jax.nn.sigmoid(b_in.astype(jnp.float32))
    g = -jnp.exp(a_log.astype(jnp.float32)) * jax.nn.softplus(
        a_in.astype(jnp.float32) + dt_bias.astype(jnp.float32))

    def to_chunks(u):
        u = u.reshape((bsz, nc, CHUNK) + u.shape[2:])
        return jnp.moveaxis(u, 3, 1)

    q, k, v = to_chunks(q), to_chunks(k), to_chunks(v)
    beta, g = to_chunks(beta), to_chunks(g)
    gc = jnp.cumsum(g, axis=-1)
    tri_incl = jnp.tril(jnp.ones((CHUNK, CHUNK), dtype=bool))
    tri_strict = jnp.tril(jnp.ones((CHUNK, CHUNK), dtype=bool), k=-1)
    diff = gc[..., :, None] - gc[..., None, :]
    decay = jnp.exp(jnp.where(tri_incl, diff, -jnp.inf))

    k_beta = k * beta[..., None]
    v_beta = v * beta[..., None]
    lower = jnp.where(tri_strict, jnp.einsum('bhncd,bhnsd->bhncs', k_beta, k) * decay, 0.0)
    eye = jnp.eye(CHUNK, dtype=jnp.float32)
    rhs = jnp.concatenate([v_beta, k_beta * jnp.exp(gc)[..., None]], axis=-1)
    sol = lax.linalg.triangular_solve(eye + lower, rhs, left_side=True, lower=True,
                                      unit_diagonal=True)
    u = sol[..., :A_HEAD_DIM]
    w = sol[..., A_HEAD_DIM:]
    qk = jnp.einsum('bhncd,bhnsd->bhncs', q, k) * decay
    q_dec = q * jnp.exp(gc)[..., None]
    k_dec = k * jnp.exp(gc[..., -1:] - gc)[..., None]
    g_last = jnp.exp(gc[..., -1])

    def step(state, inp):
        qk_n, q_dec_n, k_dec_n, u_n, w_n, gl_n = inp
        v_new = u_n - jnp.einsum('bhcd,bhdv->bhcv', w_n, state)
        o_n = (jnp.einsum('bhcd,bhdv->bhcv', q_dec_n, state)
               + jnp.einsum('bhcs,bhsv->bhcv', qk_n, v_new))
        state = state * gl_n[..., None, None] + jnp.einsum('bhcd,bhcv->bhdv', k_dec_n, v_new)
        return state, o_n

    xs = tuple(jnp.moveaxis(a, 2, 0) for a in (qk, q_dec, k_dec, u, w, g_last))
    s0 = jnp.zeros((bsz, A_HEADS, A_HEAD_DIM, A_HEAD_DIM), jnp.float32)
    _, o = lax.scan(step, s0, xs)
    o = jnp.transpose(o, (1, 0, 3, 2, 4)).reshape(bsz, t, A_HEADS, A_HEAD_DIM)
    zg = jax.nn.silu(z.astype(jnp.float32)).reshape(bsz, t, A_HEADS, A_HEAD_DIM)
    o = rms_norm_2(o, out_norm_w) * zg
    return o.reshape(bsz, t, A_INNER).astype(h.dtype) @ w_out.astype(h.dtype)

def chunk_band_attention(h, w_in, q_norm_w, k_norm_w, rel_bias, w_out):
    bsz, t, _ = h.shape
    nc = t // CHUNK
    pad = LEFT_CHUNKS * CHUNK
    proj = h @ w_in.astype(h.dtype)
    q = rms_norm_2(proj[..., :B_INNER].reshape(bsz, t, B_HEADS, B_HEAD_DIM), q_norm_w)
    k = rms_norm_2(proj[..., B_INNER:2 * B_INNER].reshape(bsz, t, B_HEADS, B_HEAD_DIM), k_norm_w)
    v = proj[..., 2 * B_INNER:3 * B_INNER].reshape(bsz, t, B_HEADS, B_HEAD_DIM)
    z = proj[..., 3 * B_INNER:]
    k_pad = jnp.pad(k, ((0, 0), (pad, 0), (0, 0), (0, 0)))
    v_pad = jnp.pad(v, ((0, 0), (pad, 0), (0, 0), (0, 0)))
    q_chunks = jnp.moveaxis(q.reshape(bsz, nc, CHUNK, B_HEADS, B_HEAD_DIM), 1, 0)

    r = jnp.arange(CHUNK)
    m = jnp.arange(BAND)
    rel = (pad + r[:, None]) - m[None, :]
    idx = jnp.clip(rel, -REL_CLIP, REL_CLIP) + REL_CLIP
    bias = rel_bias.astype(jnp.float32)[:, idx]
    scale = B_HEAD_DIM ** -0.5

    def one_chunk(args):
        n, q_n = args
        start = n * CHUNK
        k_n = lax.dynamic_slice_in_dim(k_pad, start, BAND, axis=1)
        v_n = lax.dynamic_slice_in_dim(v_pad, start, BAND, axis=1)
        s = jnp.einsum('bchd,bmhd->bhcm', q_n, k_n).astype(jnp.float32) * scale + bias
        valid = (start - pad + m) >= 0
        s = jnp.where(valid[None, None, None, :], s, -jnp.inf)
        p = jax.nn.softmax(s, axis=-1).astype(v_n.dtype)
        return jnp.einsum('bhcm,bmhd->bchd', p, v_n)

    o = lax.map(one_chunk, (jnp.arange(nc, dtype=jnp.int32), q_chunks))
    o = jnp.moveaxis(o, 0, 1).reshape(bsz, t, B_INNER)
    o = (o.astype(jnp.float32) * jax.nn.silu(z.astype(jnp.float32))).astype(h.dtype)
    return o @ w_out.astype(h.dtype)

def second_inputs(seed: int = 0) -> dict:
    key = jax.random.key(seed)
    ks = jax.random.split(key, 16)
    n_a = (DEPTH_2 + 1) // N_MIXERS_2
    n_b = DEPTH_2 // N_MIXERS_2
    f32 = jnp.float32
    x = jax.random.normal(ks[0], (BATCH, SEQ, D_MODEL), f32)
    norm_w = 1.0 + 0.02 * jax.random.normal(ks[1], (DEPTH_2, D_MODEL), f32)
    a_w_in = jax.random.normal(ks[2], (n_a, D_MODEL, 4 * A_INNER + 2 * A_HEADS), f32) * D_MODEL ** -0.5
    a_conv_w = jax.random.normal(ks[3], (n_a, CONV_K, 3 * A_INNER), f32) * CONV_K ** -0.5
    a_a_log = jnp.log(jax.random.uniform(ks[4], (n_a, A_HEADS), f32, 1.0, 16.0))
    dt = jnp.exp(jax.random.uniform(ks[5], (n_a, A_HEADS), f32, math.log(1e-3), math.log(1e-1)))
    a_dt_bias = dt + jnp.log(-jnp.expm1(-dt))
    a_out_norm_w = 1.0 + 0.02 * jax.random.normal(ks[6], (n_a, A_HEAD_DIM), f32)
    a_w_out = jax.random.normal(ks[7], (n_a, A_INNER, D_MODEL), f32) * A_INNER ** -0.5
    b_w_in = jax.random.normal(ks[8], (n_b, D_MODEL, 4 * B_INNER), f32) * D_MODEL ** -0.5
    b_q_norm_w = 1.0 + 0.02 * jax.random.normal(ks[9], (n_b, B_HEAD_DIM), f32)
    b_k_norm_w = 1.0 + 0.02 * jax.random.normal(ks[10], (n_b, B_HEAD_DIM), f32)
    b_rel_bias = 0.5 * jax.random.normal(ks[11], (n_b, B_HEADS, 2 * REL_CLIP + 1), f32)
    b_w_out = jax.random.normal(ks[12], (n_b, B_INNER, D_MODEL), f32) * B_INNER ** -0.5
    return {"x": x, "norm_w": norm_w, "a_w_in": a_w_in, "a_conv_w": a_conv_w,
            "a_a_log": a_a_log, "a_dt_bias": a_dt_bias, "a_out_norm_w": a_out_norm_w,
            "a_w_out": a_w_out, "b_w_in": b_w_in, "b_q_norm_w": b_q_norm_w,
            "b_k_norm_w": b_k_norm_w, "b_rel_bias": b_rel_bias, "b_w_out": b_w_out}

def second_block(x, norm_w, a_w_in, a_conv_w, a_a_log, a_dt_bias, a_out_norm_w, a_w_out,
              b_w_in, b_q_norm_w, b_k_norm_w, b_rel_bias, b_w_out):
    h = x
    for i in range(DEPTH_2):
        j = i // N_MIXERS_2
        hn = rms_norm_2(h, norm_w[i])
        if i % N_MIXERS_2 == 0:
            y = gated_deltanet(hn, a_w_in[j], a_conv_w[j], a_a_log[j], a_dt_bias[j],
                               a_out_norm_w[j], a_w_out[j])
        else:
            y = chunk_band_attention(hn, b_w_in[j], b_q_norm_w[j], b_k_norm_w[j],
                                     b_rel_bias[j], b_w_out[j])
        h = h + y
    return h


def setup_inputs(seed=0):
    out = dict(first_inputs(seed))
    for name, value in second_inputs(seed + 1).items():
        if name != "x":
            out[name + "_2"] = value
    return out


def reference(
    x, c, w_mod, b_mod, pool_w_in, pool_w_grp, pool_scale, pool_w_out, gla_w_in, gla_fwd_w1,
    gla_fwd_w2, gla_fwd_b, gla_bwd_w1, gla_bwd_w2, gla_bwd_b, gla_norm_g, gla_w_out, attn_w_in,
    attn_q_norm_g, attn_k_norm_g, attn_w_out, final_norm_g, norm_w_2, a_w_in_2, a_conv_w_2,
    a_a_log_2, a_dt_bias_2, a_out_norm_w_2, a_w_out_2, b_w_in_2, b_q_norm_w_2, b_k_norm_w_2,
    b_rel_bias_2, b_w_out_2,
):
    x = first_block(
        x, c, w_mod, b_mod, pool_w_in, pool_w_grp, pool_scale, pool_w_out, gla_w_in, gla_fwd_w1,
        gla_fwd_w2, gla_fwd_b, gla_bwd_w1, gla_bwd_w2, gla_bwd_b, gla_norm_g, gla_w_out,
        attn_w_in, attn_q_norm_g, attn_k_norm_g, attn_w_out, final_norm_g,
    )
    return second_block(
        x, norm_w_2, a_w_in_2, a_conv_w_2, a_a_log_2, a_dt_bias_2, a_out_norm_w_2, a_w_out_2,
        b_w_in_2, b_q_norm_w_2, b_k_norm_w_2, b_rel_bias_2, b_w_out_2,
    )


_drawn_inputs = setup_inputs


def setup_inputs(seed=0):
    import zlib

    import numpy as np

    out = dict(_drawn_inputs(seed))
    spreads = {}
    factors = {'b_mod': 3.402,
     'norm_w_2': 3.201,
     'a_out_norm_w_2': 5.351,
     'b_q_norm_w_2': 8.0,
     'b_k_norm_w_2': 8.0}
    for name, (base, spread) in spreads.items():
        noise = np.random.default_rng([zlib.crc32(name.encode()), seed]).standard_normal(out[name].shape)
        drawn = base * np.exp(spread * noise) if base else spread * noise
        out[name] = __import__('jax').numpy.asarray(drawn.astype(out[name].dtype))
    for name, factor in factors.items():
        out[name] = (out[name] * factor).astype(out[name].dtype)
    return out
```

```python
from contextlib import ExitStack

import numpy as np
import concourse.bass as bass
from concourse import mybir

F32 = mybir.dt.float32
F32R = mybir.dt.float32r
ACT = mybir.ActivationFunctionType
ALU = mybir.AluOpType

P = 128
D = 2048
T = 256
KT = D // P
GC = 512
GM = GC // P
SLAB_K = 2
SLABS = KT // SLAB_K
RAW_SLOTS = 4
HL_SLOTS = 8
AHEAD = 15
EPS = 1e-6
HEADS = 16
CHUNK = 64
BATCH = 4
WINDOWS = (2, 4, 8, 16)
PAD = 8
UW = T + 2 * PAD
REL = 2 * T + 1
MASKED = -3e38
MOD_SLOTS = 6
PAIRS = BATCH * (T + P)
GATES = 2 * KT

G_UG, G_GRP, G_WOUT, G_A, G_AOUT, G_B, G_BOUT, G_END = 0, 8, 12, 16, 32, 36, 52, 56
GRP_SLABS = GM // SLAB_K
N_GRP = 8 * SLABS
N_WOUT = N_GRP + 4 * GRP_SLABS
N_SLABS = N_WOUT + (G_END - G_WOUT) * SLABS

O_H, O_POOLED, O_Z = KT, KT + 4, KT + 8
O_A = O_Z + KT
O_AO = O_A + 4
O_B = O_AO + KT

V_C, V_BMOD, V_PSC, V_FG, V_NW0, V_NW1, V_CONV = 0, 16, 64, 80, 96, 112, 128
V_ONW, V_QNW, V_KNW, V_ALOG, V_DTB, V_EDGE, V_END = 320, 321, 322, 323, 339, 355, 419
C_ID, C_GT, C_ONE, C_UP, C_BD, C_M1, C_M2, C_EX, C_END = 0, 128, 256, 384, 640, 768, 896, 1024, 1152


class Num:

    def __init__(self, c, var=None, mul=0):
        self.c, self.var, self.mul = c, var, mul

    def __add__(self, k):
        return Num(self.c + k, self.var, self.mul)

    def times(self, k):
        return Num(self.c * k, self.var, self.mul * k)

    @property
    def v(self):
        return self.c if self.var is None or self.mul == 0 else self.var * self.mul + self.c


class Own:

    def __init__(self, main):
        self.main, self.count, self.steps, self.loop_of = main, {}, [], None

    def also(self, sem):
        self.count[sem.name] = self.count.get(sem.name, Num(0)) + 1
        return sem

    def up(self, sem):
        self.also(sem)
        self.steps.append((sem, self.count[sem.name]))
        return sem

    def last(self, k=1):
        sem, n = self.steps[-k]
        return sem, n.v

    def reset(self):
        self.steps = [(self.main, self.count[self.main.name])]

    def enter(self, i, per):
        for s, k in per.items():
            self.count[s.name] = Num(self.count.get(s.name, Num(0)).c, i, k)
        self.loop_of = (dict(self.count), per)
        self.reset()

    def leave(self, times):
        was, per = self.loop_of
        rose = {n: self.count[n].c - was.get(n, Num(0)).c for n in self.count}
        told = {s.name: k for s, k in per.items()}
        assert {n: k for n, k in rose.items() if k} == told, (rose, told)
        for n in self.count:
            self.count[n] = Num(was[n].c + was[n].mul * times)
        self.reset()


def slab_of(g):
    return g.times(SLABS) + (N_WOUT - G_WOUT * SLABS)


def program(nc, weights, mod_w, x_t, vecs_d, consts_d, w_ab_d, bias_d, out_d):
    ctx = ExitStack()
    with ctx:
        top = [nc.sbuf_base + (-nc.sbuf_base) % 64]

        def at(name, shape, dtype, offset=None):
            size = int(np.prod(shape[1:])) * 4
            if offset is None:
                offset = top[0]
                top[0] += size + (-size) % 32
            return nc.alloc_sbuf_tensor_at(name, shape, dtype, offset=offset)

        def sem(name):
            return ctx.enter_context(nc.semaphore(name))

        raw = at("raw", [P, RAW_SLOTS, SLAB_K * GC], F32)
        w_hi = at("w_hi", [P, HL_SLOTS, SLAB_K * GC], F32R)
        w_lo = at("w_lo", [P, HL_SLOTS, SLAB_K * GC], F32R)
        a_at = top[0]
        a_hi = at("a_hi", [P, KT, T], F32R)
        a_lo = at("a_lo", [P, KT, T], F32R)
        b_at = top[0]
        b_hi = at("b_hi", [P, KT, T], F32R)
        b_lo = at("b_lo", [P, KT, T], F32R)
        vo_at = top[0]
        vo = at("vo", [P, KT, T], F32)
        x_at = top[0]
        xres = at("xres", [P, KT, T], F32)
        t0 = at("t0", [P, 4 * UW], F32)
        t1 = at("t1", [P, 4 * UW], F32)
        t2 = at("t2", [P, 4 * UW], F32)
        t34_at = top[0]
        t3 = at("t3", [P, 4 * T], F32)
        t4 = at("t4", [P, 4 * T], F32)
        vecs = at("vecs", [P, V_END], F32)
        consts = at("consts", [P, C_END], F32)
        r1 = at("r1", [P, T], F32)
        r2 = at("r2", [P, T], F32)
        silu_c = at("silu_c", [P, KT], F32)
        modv = at("modv", [P, 3 * KT], F32)
        small = at("small", [P, 4], F32)
        decay = at("decay", [P, 2 * HEADS], F32)
        beta = at("beta", [P, 2 * HEADS], F32)
        ab_t = at("ab_t", [P, 5, 2 * HEADS], F32)
        beta_now = at("beta_now", [P, 2, BATCH], F32)
        row_max = at("row_max", [P, 2, BATCH], F32)
        row_sum = at("row_sum", [P, 2, BATCH], F32)
        conv_now = at("conv_now", [P, GM * 4], F32)
        assert top[0] <= nc.sbuf_usable_end, top[0]
        mod_ring = at("mod_ring", [P, MOD_SLOTS, D], F32, b_at)
        mod_acc = at("mod_acc", [P, D], F32, t34_at)
        q_n = at("q_n", [P, 4 * T], F32, a_at)
        k_n = at("k_n", [P, 4 * T], F32, a_at + 4096)
        dec_t = at("dec_t", [P, PAIRS], F32, a_at + 8192)
        gu_t = at("gu_t", [P, PAIRS], F32, a_at + 14336)
        l_t = at("l_t", [P, PAIRS], F32, a_at + 20480)
        a_t = at("a_t", [P, PAIRS], F32, a_at + 26624)
        ab_raw = at("ab_raw", [P, KT * 2 * HEADS], F32, a_at + 20480)
        ab_hi = at("ab_hi", [P, KT * 2 * HEADS], F32R, a_at + 22528)
        ab_lo = at("ab_lo", [P, KT * 2 * HEADS], F32R, a_at + 24576)
        blk = at("blk", [P, 32, 32], F32, a_at)
        inv = at("inv", [P, 32, 32], F32, a_at + 4096)
        inv_t = at("inv_t", [P, 32, 32], F32, a_at + 8192)
        prod = at("prod", [P, 256], F32, a_at + 12288)
        l_x = at("l_x", [P, PAIRS], F32, x_at)
        a_x = at("a_x", [P, PAIRS], F32, x_at + 6144)
        xc = at("xc", [P, 2 * BATCH * 32], F32, x_at + 12288)
        yc = at("yc", [P, 2 * BATCH * 32], F32, x_at + 13312)
        p_t = at("p_t", [P, PAIRS], F32, vo_at)
        p_tt = at("p_tt", [P, PAIRS], F32, vo_at + 4 * PAIRS)
        v_n = at("v_n", [P, 2, GC], F32, vo_at + 8 * PAIRS)
        acc = ctx.enter_context(nc.psum_tensor("acc", [P, 2, 4 * T], F32))
        misc = ctx.enter_context(nc.psum_tensor("misc", [P, 2048], F32))

        ident = consts[:, C_ID:C_ID + P]
        exchange = consts[:, C_EX:C_EX + P]
        ones = consts[:, C_ONE:C_ONE + P]
        eps = small[:, 0:1]
        log_q = small[:, 1:2]

        def tiles(t, n=4, w=T):
            return t[:, 0:n * w].rearrange("p (k t) -> p k t", k=n)

        l_d = [nc.dram_tensor(f"l{k}_d", (P, HEADS * w), F32).ap() for k, w in ((0, T), (1, P))]
        a_d = [nc.dram_tensor(f"a{k}_d", (P, HEADS * w), F32).ap() for k, w in ((0, T), (1, P))]
        inv_d = [nc.dram_tensor(f"inv{k}_d", (P, 2, HEADS, 32), F32).ap() for k in (0, 1)]
        x_d = nc.dram_tensor("x_d", (P, KT, T), F32).ap()

        s_raw = [sem(f"s_raw{i}") for i in range(RAW_SLOTS)]
        s_hi = sem("s_hi")
        s_lo = sem("s_lo")
        s_gate = sem("s_gate")
        s_used = sem("s_used")
        s_free = sem("s_free")
        s_opnd = sem("s_opnd")
        s_tmp = sem("s_tmp")
        s_rnd = sem("s_rnd")
        s_mod = [sem(f"s_mod{i}") for i in range(MOD_SLOTS)]
        s_mod_used = sem("s_mod_used")
        s_mod_sum = sem("s_mod_sum")
        s_vec = sem("s_vec")
        s_con = sem("s_con")
        s_x = sem("s_x")
        s_shift = sem("s_shift")
        s_silu_c = sem("s_silu_c")
        s_sq = sem("s_sq")
        s_sums = sem("s_sums")
        s_stat = sem("s_stat")
        s_root = sem("s_root")
        s_var2 = sem("s_var2")
        s_act_read = sem("s_act_read")
        s_x1 = sem("s_x1")
        s_eps = sem("s_eps")
        s_pads = sem("s_pads")
        s_dve = sem("s_dve")
        s_act = sem("s_act")
        s_outs = [sem(f"s_outs{j}") for j in range(4)]
        s_ab = sem("s_ab")
        s_ab_hi = sem("s_ab_hi")
        s_ab_lo = sem("s_ab_lo")
        s_ab_mm = sem("s_ab_mm")
        s_ab_act = sem("s_ab_act")
        s_ab_dve = sem("s_ab_dve")
        s_tap = sem("s_tap")
        s_sq2 = sem("s_sq2")
        s_nrm = sem("s_nrm")
        s_rinv = sem("s_rinv")
        s_qkn = sem("s_qkn")
        s_gu = sem("s_gu")
        s_dm = sem("s_dm")
        s_e = sem("s_e")
        s_em = sem("s_em")
        s_kk = sem("s_kk")
        s_qk = sem("s_qk")
        s_l = sem("s_l")
        s_a = sem("s_a")
        s_ld = [sem("s_ld0"), sem("s_ld1")]
        s_ad = [sem("s_ad0"), sem("s_ad1")]
        s_blk = sem("s_blk")
        s_inv = sem("s_inv")
        s_invd = sem("s_invd")
        s_xd = sem("s_xd")
        s_xb = sem("s_xb")
        s_vt = sem("s_vt")
        s_lx = [sem("s_lx0"), sem("s_lx1")]
        s_ax = [sem("s_ax0"), sem("s_ax1")]
        s_cx = [sem("s_cx0"), sem("s_cx1")]
        s_dense = sem("s_dense")
        s_solve_pe = sem("s_solve_pe")
        s_solve_act = sem("s_solve_act")
        s_solve_dve = sem("s_solve_dve")
        s_on = sem("s_on")
        s_zs = sem("s_zs")

        s_bias = sem("s_bias")
        s_bn = sem("s_bn")
        s_score = sem("s_score")
        s_max = sem("s_max")
        s_prob = sem("s_prob")
        s_pn = sem("s_pn")
        s_pt = sem("s_pt")
        s_ptc_act = sem("s_ptc_act")
        s_ptc_dve = sem("s_ptc_dve")
        s_vn = sem("s_vn")
        s_pv = sem("s_pv")
        s_zb = sem("s_zb")
        s_y = sem("s_y")

        block = ctx.enter_context(nc.Block())

        @block.sync
        def _(sp):
            sp.dma_start(vecs[:], vecs_d).then_inc(s_vec, 16)
            for i in range(2 * KT):
                if i >= MOD_SLOTS:
                    sp.wait_ge(s_mod_used, i - MOD_SLOTS + 1)
                sp.dma_start(mod_ring[:, i % MOD_SLOTS], mod_w[i]).then_inc(s_mod[i % MOD_SLOTS], 16)
                if i == 1:
                    sp.dma_start(xres[:], x_t).then_inc(s_x, 16)

            def piece(q, slot, var=None, mul=0):
                before = q - RAW_SLOTS
                if before >= 0 or var is not None:
                    if before % 3 == 2:
                        sp.wait_ge(s_gate, Num(before // 3 + 1, var, mul // 3).v)
                    else:
                        sp.wait_ge(s_lo, Num(before // 3 * 2 + before % 3 + 1, var, mul // 3 * 2).v)
                land(Num(q, var, mul), slot)

            def land(q, slot):
                sp.dma_start(raw[:, slot], weights[bass.ds(q.times(P).v, P), :]).then_inc(s_raw[slot], 16)

            for q in range(12):
                piece(q, q % RAW_SLOTS)
            with sp.Fori(1, 8) as i:
                for q in range(12):
                    piece(q, q % RAW_SLOTS, i, 12)
            for q in range(12 * 8, 12 * 8 + 4):
                piece(q, q % RAW_SLOTS)
            with sp.Fori(N_GRP // 4 + 1, N_SLABS // 4) as i:
                for k in range(4):
                    sp.wait_ge(s_lo, Num(k - 3, i, 4).v)
                    land(Num(GATES + k, i, 4), k)
            for j in range(4):
                sp.wait_ge(s_y, j + 1)
                sp.dma_start(out_d[:, 4 * j:4 * j + 4], vo[:, 4 * j:4 * j + 4]).then_inc(s_outs[j], 16)
            for j in range(4):
                sp.wait_ge(s_outs[j], 16)

        @block.gpsimd
        def _(pool):
            pool.dma_start(consts[:], consts_d).then_inc(s_con, 16)
            pool.memset(small[:, 0:1], EPS).then_inc(s_eps, 1)
            pool.memset(small[:, 1:2], -0.5 * float(np.log(P))).then_inc(s_eps, 1)
            pool.wait_ge(s_stat, 1)
            pool.memset(t0[:], 0.0).then_inc(s_pads, 1)
            pool.wait_ge(s_opnd, O_A)
            pool.dma_start(x_d, xres[:]).then_inc(s_xd, 16)
            pool.dma_start(ab_raw[:], w_ab_d.rearrange("p k c -> p (k c)")).then_inc(s_ab, 16)

            up = consts[:, C_UP:C_UP + T]
            up_tile = up[:, 0:P].unsqueeze(1).to_broadcast([P, BATCH, P])
            pool.wait_ge(s_ab_dve, 5)
            for i in range(4):
                if i:
                    pool.wait_ge(s_dm, i)
                for h in range(BATCH):
                    for b, w, at_ in ((0, T, h * T), (1, P, BATCH * T + h * P)):
                        col = b * HEADS + BATCH * i + h
                        last = pool.tensor_scalar(gu_t[:, at_:at_ + w], up[:, 0:w], decay[:, col:col + 1], None,
                                                  ALU.mult)
                        last.then_inc(s_gu, 1)
                if i:
                    for k in range(2):
                        pool.wait_ge(s_ld[k], 16 * i)
                        pool.wait_ge(s_ad[k], 16 * i)
                pool.wait_ge(s_e, i + 1)
                for view in (dec_t[:, 0:BATCH * T].rearrange("p (h t) -> p h t", h=BATCH)[:, :, 0:P],
                             dec_t[:, BATCH * T:PAIRS].rearrange("p (h t) -> p h t", h=BATCH)):
                    pool.tensor_tensor(view, view, up_tile, ALU.mult).then_inc(s_em, 1)
                for tile, done, dst, sems in ((l_t, s_l, l_d, s_ld), (a_t, s_a, a_d, s_ad)):
                    pool.wait_ge(done, i + 1)
                    pool.dma_start(dst[0][:, BATCH * T * i:BATCH * T * (i + 1)], tile[:, 0:BATCH * T]
                                   ).then_inc(sems[0], 16)
                    pool.dma_start(dst[1][:, BATCH * P * i:BATCH * P * (i + 1)], tile[:, BATCH * T:PAIRS]
                                   ).then_inc(sems[1], 16)

            for k in range(2):
                pool.wait_ge(s_ld[k], 64)
            for half in range(2):
                for b in range(4):
                    at_ = (half * 4 + b) * HEADS
                    src = l_d[half].rearrange("s (h t) -> h s t", h=HEADS)
                    pool.dma_start(blk[at_:at_ + HEADS], src[:, 32 * b:32 * b + 32, 32 * b:32 * b + 32]
                                   ).then_inc(s_blk, 16)
            pool.wait_ge(s_inv, 1)
            for k, tile in enumerate((inv, inv_t)):
                for half in range(2):
                    for b in range(4):
                        at_ = (half * 4 + b) * HEADS
                        dst = inv_d[k][32 * b:32 * b + 32, half].rearrange("s h t -> h s t")
                        pool.dma_start(dst, tile[at_:at_ + HEADS]).then_inc(s_invd, 16)
            pool.wait_ge(s_invd, 16 * 16)
            for k in range(2):
                pool.wait_ge(s_ad[k], 64)
            pool.wait_ge(s_xd, 16)

            block_mask = consts[:, C_BD:C_BD + P].rearrange("p (b t) -> p b t", b=4)

            def dense(out, compact):
                o = out[:, 0:8 * P].rearrange("p (n b t) -> p n b t", n=8, b=4)
                c = compact[:].rearrange("p (n t) -> p n t", n=8).unsqueeze(2).to_broadcast([P, 8, 4, 32])
                pool.tensor_tensor(o, c, block_mask.unsqueeze(1).to_broadcast([P, 8, 4, 32]), ALU.mult
                                   ).then_inc(s_dense, 1)

            def off_diagonal(col):
                mask = consts[:, col:col + P].unsqueeze(1).to_broadcast([P, BATCH, P])
                for half in range(2):
                    src = (l_x[:, 0:BATCH * T].rearrange("p (h t) -> p h t", h=BATCH)[:, :, 0:P] if half == 0 else
                           l_x[:, BATCH * T:PAIRS].rearrange("p (h t) -> p h t", h=BATCH))
                    out = t2[:, half * BATCH * P:(half + 1) * BATCH * P].rearrange("p (h t) -> p h t", h=BATCH)
                    pool.tensor_tensor(out, src, mask, ALU.mult).then_inc(s_dense, 1)

            for j in range(4):
                if j:
                    pool.wait_ge(s_solve_pe, 8 * j - 2)
                for k, (a, b) in enumerate(((0, BATCH * T), (BATCH * T, PAIRS))):
                    w = b - a
                    pool.dma_start(l_x[:, a:b], l_d[k][:, w * j:w * (j + 1)]).then_inc(s_lx[k], 16)
                if j:
                    pool.wait_ge(s_dense, 6 * j)
                for k, tile in enumerate((xc, yc)):
                    src = inv_d[k][:, :, BATCH * j:BATCH * (j + 1), :].rearrange("s a h t -> s a (h t)")
                    pool.dma_start(tile[:].rearrange("p (a c) -> p a c", a=2), src).then_inc(s_cx[k], 16)
                for k in range(2):
                    pool.wait_ge(s_cx[k], 16 * (j + 1))
                if j:
                    pool.wait_ge(s_solve_pe, 8 * j - 1)
                else:
                    pool.wait_ge(s_vt, 4)
                dense(t1, xc)
                dense(t0, yc)
                for k in range(2):
                    pool.wait_ge(s_lx[k], 16 * (j + 1))
                off_diagonal(C_M1)
                if j:
                    pool.wait_ge(s_solve_pe, 8 * j)
                for k, (a, b) in enumerate(((0, BATCH * T), (BATCH * T, PAIRS))):
                    w = b - a
                    pool.dma_start(a_x[:, a:b], a_d[k][:, w * j:w * (j + 1)]).then_inc(s_ax[k], 16)
                pool.wait_ge(s_solve_pe, 8 * j + 1)
                off_diagonal(C_M2)
            pool.wait_ge(s_solve_pe, 32)
            pool.dma_start(xres[:], x_d).then_inc(s_xb, 16)
            for j in range(4):
                if j:
                    pool.wait_ge(s_score, j)
                else:
                    pool.wait_ge(s_x1, 5)
                src = bass.AP(tensor=bias_d.tensor, offset=bias_d.offset + BATCH * REL * j + 1,
                              ap=[[1, P], [REL, BATCH], [1, T]])
                pool.dma_start(t4[:].rearrange("p (h s) -> p h s", h=BATCH), src).then_inc(s_bias, 16)

        @block.tensor
        def _(pe):
            def by_channel(out, kt, end, wh, wl, xh, xl):
                for m in range(GM):
                    to = out[:, m * T:(m + 1) * T]
                    ch = slice(m * P, (m + 1) * P)
                    nc.tensor.matmul(to, wh[:, ch], xh, start=kt == 0 and m % 2 == 0, stop=False,
                                     skip_group_check=True)
                    nc.tensor.matmul(to, wh[:, ch], xl, start=False, stop=False, skip_group_check=True)
                    last = nc.tensor.matmul(to, wl[:, ch], xh, start=False, stop=end and m % 2 == 1,
                                            skip_group_check=True)
                return last

            def by_token(out, kt, end, wh, wl, xh, xl):
                for half in range(2):
                    to, t = out[:, half * GC:(half + 1) * GC], slice(half * P, (half + 1) * P)
                    nc.tensor.matmul(to, xh[:, t], wh, start=kt == 0, stop=False)
                    nc.tensor.matmul(to, xh[:, t], wl, start=False, stop=False)
                    last = nc.tensor.matmul(to, xl[:, t], wh, start=False, stop=end)
                return last

            def group(free, n0, par, slot0, hi, lo, kt0=0, slabs=SLABS, ready=None,
                      fillers=None, products=by_channel):
                if free is not None:
                    pe.wait_ge(s_free, free.v)
                for s in range(slabs):
                    slot = (slot0 + s) % HL_SLOTS
                    pe.wait_ge(s_lo, (n0 + (s + 1)).v)
                    for kk in range(SLAB_K):
                        kt = s * SLAB_K + kk
                        if ready and (kt == 0 or ready(kt) != ready(kt - 1)):
                            pe.wait_ge(s_opnd, ready(kt))
                        row = slice(kk * GC, (kk + 1) * GC)
                        last = products(acc[:, par], kt, kt == slabs * SLAB_K - 1, w_hi[:, slot, row],
                                        w_lo[:, slot, row], hi[:, kt0 + kt], lo[:, kt0 + kt])
                    last.then_inc(s_used, 1)
                    if fillers and s in fillers:
                        fillers[s]()

            def partition_sums(ready, src, out):
                pe.wait_ge(s_sums, ready)
                for k in range(4):
                    last = nc.tensor.matmul(out, ones, src[:, k * T:(k + 1) * T],
                                            start=(k == 0), stop=(k == 3))
                last.then_inc(s_stat, 1)

            def mod_sums(pieces):
                for m in range(KT):
                    col = 512 * (m // (KT // pieces)) + m
                    last = nc.tensor.matmul(misc[:, col:col + 1], mod_acc[:, m * P:(m + 1) * P],
                                            ones[:, 0:1], start=True, stop=True)
                    if (m + 1) % (KT // pieces) == 0:
                        last.then_inc(s_mod_sum, 1)

            pe.wait_ge(s_con, 16)
            partition_sums(1, t0, misc[:, 0:T])
            pe.wait_ge(s_mod_used, KT)
            pe.wait_ge(s_root, 1)
            mod_sums(1)
            pe.wait_ge(s_mod_used, 2 * KT)
            pe.wait_ge(s_shift, 1)
            mod_sums(4)

            group(None, Num(0), 0, 0, a_hi, a_lo, ready=lambda kt: kt + 1)
            group(None, Num(SLABS), 1, 0, a_hi, a_lo)
            with pe.Fori(1, 4) as i:
                for k in range(2):
                    group(Num(k - 1, i, 2), Num(k * SLABS, i, 2 * SLABS), k, 0, a_hi, a_lo)
            pe.wait_ge(s_gate, GATES)
            mod_sums(1)
            for j in range(4):
                group(Num(G_GRP + j - 1), Num(N_GRP + j * GRP_SLABS), j % 2, j * GRP_SLABS, b_hi, b_lo,
                      kt0=4 * j, slabs=GRP_SLABS, ready=lambda kt: O_H + j + 1)
            with pe.Fori(0, 2) as i:
                for k in range(2):
                    g = Num(G_WOUT + k, i, 2)
                    group(g + (-1), slab_of(g), k, N_WOUT % HL_SLOTS, a_hi, a_lo,
                          ready=lambda kt: O_POOLED + kt // 4 + 1)
            partition_sums(6, t3, misc[:, 0:T])
            partition_sums(7, t4, misc[:, 512:512 + T])

            def operand_b(kt):
                return O_Z + kt + 1

            def pairs(step, lhs, rhs, done, also=None):
                for h in range(BATCH):
                    k = h * T
                    nc.tensor.matmul(misc[:, k:k + T], lhs(h, 0), rhs(h, 0, T), start=True, stop=also is None)
                    if also:
                        nc.tensor.matmul(misc[:, k + P:k + T], also, rhs(h, 1, P), start=False, stop=True)
                    k = BATCH * T + h * P
                    last = nc.tensor.matmul(misc[:, k:k + P], lhs(h, 1), rhs(h, 1, P), start=True, stop=True)
                last.then_inc(done, 1)

            def head_sums(n, src, at_=0):
                pe.wait_ge(s_sq2, n.v)
                for h in range(BATCH):
                    last = nc.tensor.matmul(misc[:, at_ + h * T:at_ + (h + 1) * T], ones, src[:, h * T:(h + 1) * T],
                                            start=True, stop=True)
                last.then_inc(s_nrm, 1)

            def log_decays(i):
                pe.wait_ge(s_rinv, Num(1, i, 2).v)
                pe.wait_ge(s_gu, Num(8, i, 8).v)
                later = consts[:, C_GT:C_GT + P]

                def rhs(h, half, w):
                    k = h * T if half == 0 else BATCH * T + h * P
                    return gu_t[:, k:k + w]

                pairs(i, lambda h, half: later, rhs, s_dm, also=ones)

            def key_products(i, q, done):
                def rhs(h, half, w):
                    return q[:, h * T + half * P:h * T + half * P + w]

                pairs(i, lambda h, half: k_n[:, h * T + half * P:h * T + half * P + P], rhs, done)

            def key_key(i):
                pe.wait_ge(s_qkn, Num(2, i, 2).v)
                key_products(i, k_n, s_kk)

            def key_query(i):
                pe.wait_ge(s_l, Num(1, i, 1).v)
                key_products(i, q_n, s_qk)

            g = Num(G_A)
            group(g + (-1), slab_of(g), 0, 0, b_hi, b_lo, ready=operand_b)
            pe.wait_ge(s_ab_lo, 1)
            for half in range(2):
                out = misc[:, 1536 + half * 2 * HEADS:1536 + (half + 1) * 2 * HEADS]
                for kt in range(KT):
                    xh, xl = (x[:, kt, half * P:(half + 1) * P] for x in (b_hi, b_lo))
                    wh, wl = (w[:, kt * 2 * HEADS:(kt + 1) * 2 * HEADS] for w in (ab_hi, ab_lo))
                    nc.tensor.matmul(out, xh, wh, start=kt == 0, stop=False)
                    nc.tensor.matmul(out, xh, wl, start=False, stop=False)
                    last = nc.tensor.matmul(out, xl, wh, start=False, stop=kt == KT - 1)
            last.then_inc(s_ab_mm, 1)
            with pe.Fori(0, 4) as i:
                g = Num(G_A + 1, i, 2)
                group(g + (-1), slab_of(g), 1, 0, b_hi, b_lo, fillers={
                    3: lambda: head_sums(Num(1, i, 2), t2), 5: lambda: log_decays(i)})
                g = g + 1
                group(g + (-1), slab_of(g), 0, 0, b_hi, b_lo, fillers={
                    3: lambda: head_sums(Num(2, i, 2), t2), 5: lambda: key_key(i), 6: lambda: key_query(i)})
            for k in range(9, 12):
                g = Num(G_A + k)
                group(g + (-1), slab_of(g), k % 2, 0, b_hi, b_lo)

            def tile_of(t, half, h):
                k = (half * BATCH + h) * P
                return t[:, k:k + P]

            def eight(bank, lhs, rhs):
                for half in range(2):
                    for h in range(BATCH):
                        k = 1024 * bank + (half * BATCH + h) * P
                        last = nc.tensor.matmul(misc[:, k:k + P], tile_of(lhs, half, h), tile_of(rhs, half, h),
                                                start=True, stop=True)
                return last

            def value(j, h, half):
                return vo[:, BATCH * j + h, half * P:(half + 1) * P]

            def solve(j, step):
                done = None
                if step == 0:
                    pe.wait_ge(s_dense, 6 * j + 4)
                    if j:
                        pe.wait_ge(s_solve_act, 6 * j)
                    done = eight(0, t2, t1)
                elif step == 1:
                    pe.wait_ge(s_solve_act, 6 * j + 1)
                    eight(1, t3, t0)
                    done = eight(0, t0, t3)
                elif step == 2:
                    pe.wait_ge(s_solve_dve, 3 * j + 1)
                    pe.wait_ge(s_dense, 6 * j + 6)
                    eight(0, t2, t1)
                    for h in range(BATCH):
                        for half in range(2):
                            k = 1024 + h * T + half * P
                            done = nc.tensor.transpose(misc[:, k:k + P], value(j, h, half), ident)
                elif step == 3:
                    pe.wait_ge(s_solve_act, 6 * j + 3)
                    done = eight(1, t3, t0)
                elif step == 4:
                    pe.wait_ge(s_solve_dve, 3 * j + 2)
                    for h in range(BATCH):
                        done = nc.tensor.matmul(misc[:, h * P:(h + 1) * P], tile_of(t0, 0, h), value(j, h, 0),
                                                start=True, stop=True)
                elif step == 5:
                    pe.wait_ge(s_solve_act, 6 * j + 4)
                    for h in range(BATCH):
                        done = nc.tensor.matmul(misc[:, 512 + h * P:512 + (h + 1) * P],
                                                l_x[:, h * T + P:(h + 1) * T], value(j, h, 0),
                                                start=True, stop=True)
                elif step == 6:
                    pe.wait_ge(s_solve_dve, 3 * j + 3)
                    for h in range(BATCH):
                        done = nc.tensor.matmul(misc[:, h * P:(h + 1) * P], tile_of(t0, 1, h), value(j, h, 1),
                                                start=True, stop=True)
                else:
                    pe.wait_ge(s_solve_act, 6 * j + 5)
                    for k in range(2):
                        pe.wait_ge(s_ax[k], 16 * (j + 1))
                    for h in range(BATCH):
                        nc.tensor.matmul(misc[:, h * T:(h + 1) * T], value(j, h, 0), a_x[:, h * T:(h + 1) * T],
                                         start=True, stop=False)
                        k = BATCH * T + h * P
                        done = nc.tensor.matmul(misc[:, h * T + P:(h + 1) * T], value(j, h, 1), a_x[:, k:k + P],
                                                start=False, stop=True)
                done.then_inc(s_solve_pe, 1)

            for j in range(4):
                g = Num(G_A + 12 + j)
                fill = {s: (lambda s=s: solve(j, s)) for s in range(8)}
                if j:
                    fill[4] = lambda: (solve(j, 4), head_sums(Num(8 + j), t4, 1024))
                group(g + (-1), slab_of(g), j % 2, 0, b_hi, b_lo, fillers=fill)
            for j in range(4):
                g = Num(G_AOUT + j)
                group(g + (-1), slab_of(g), j % 2, 0, a_hi, a_lo, ready=lambda kt: O_A + kt // 4 + 1,
                      fillers={0: lambda: head_sums(Num(12), t4, 1024)} if j == 0 else None)
            partition_sums(10, t3, misc[:, 0:T])

            def scores(i):
                pe.wait_ge(s_bn, Num(2, i, 2).v)
                pe.wait_ge(s_bias, Num(16, i, 16).v)
                for h in range(BATCH):
                    k = h * T
                    nc.tensor.matmul(misc[:, k:k + T], t2[:, k + P:k + T], t0[:, k:k + T],
                                     start=True, stop=False)
                    nc.tensor.matmul(misc[:, k:k + T], exchange, t4[:, k:k + T], start=False, stop=True)
                    at_ = BATCH * T + h * P
                    nc.tensor.matmul(misc[:, at_:at_ + P], t2[:, k:k + P], t0[:, k:k + P],
                                     start=True, stop=False)
                    last = nc.tensor.matmul(misc[:, at_:at_ + P], exchange, t4[:, k + P:k + T],
                                            start=False, stop=True)
                last.then_inc(s_score, 1)

            def transposed(i):
                pe.wait_ge(s_pn, Num(1, i, 1).v)
                for h in range(BATCH):
                    k, at_ = h * T, BATCH * T + h * P
                    nc.tensor.transpose(misc[:, k:k + P], p_t[:, at_:at_ + P], ident)
                    nc.tensor.transpose(misc[:, k + P:k + T], p_t[:, k:k + P], ident)
                    last = nc.tensor.transpose(misc[:, at_:at_ + P], p_t[:, k + P:k + T], ident)
                last.then_inc(s_pt, 1)

            def attended(i):
                pe.wait_ge(s_vn, Num(1, i, 1).v)
                pe.wait_ge(s_ptc_act, Num(1, i, 1).v)
                pe.wait_ge(s_ptc_dve, Num(1, i, 1).v)
                for h in range(BATCH):
                    k, at_ = h * T, BATCH * T + h * P
                    nc.tensor.matmul(misc[:, k:k + T], v_n[:, 0, h * P:(h + 1) * P], p_tt[:, k:k + T],
                                     start=True, stop=False)
                    last = nc.tensor.matmul(misc[:, k + P:k + T], v_n[:, 1, h * P:(h + 1) * P],
                                            p_tt[:, at_:at_ + P], start=False, stop=True)
                last.then_inc(s_pv, 1)

            with pe.Fori(0, 4) as i:
                g = Num(G_B, i, 4)
                group(g + (-1), slab_of(g), 0, 0, b_hi, b_lo, ready=lambda kt: O_AO + kt + 1)
                g = g + 1
                group(g + (-1), slab_of(g), 1, 0, b_hi, b_lo, fillers={
                    3: lambda: head_sums(Num(13, i, 2), t1)})
                g = g + 1
                group(g + (-1), slab_of(g), 0, 0, b_hi, b_lo, products=by_token, fillers={
                    3: lambda: head_sums(Num(14, i, 2), t1), 6: lambda: scores(i)})
                g = g + 1
                group(g + (-1), slab_of(g), 1, 0, b_hi, b_lo, fillers={
                    4: lambda: transposed(i), 6: lambda: attended(i)})
            for j in range(4):
                g = Num(G_BOUT + j)
                group(g + (-1), slab_of(g), j % 2, 0, a_hi, a_lo, ready=lambda kt: O_B + kt // 4 + 1)

        def stream_of(n):
            return n + GATES if n.var is not None or n.c >= N_GRP else Num(n.c // 2 * 3 + n.c % 2)

        def wide(t, k0=0):
            return t[:, k0:k0 + 4].rearrange("p k t -> p (k t)")

        def halves_of_pairs():
            return (1, 0, T), (0, BATCH * T, P)

        @block.scalar
        def _(act):
            own = Own(s_hi)

            def hi_parts(n, count):
                for k in range(count):
                    m = n + k
                    if m.var is None and m.c >= N_SLABS:
                        return
                    q = stream_of(m)
                    act.wait_ge(s_raw[q.c % RAW_SLOTS],
                                Num(16 * (q.c // RAW_SLOTS + 1), q.var, 16 * q.mul // RAW_SLOTS).v)
                    if m.var is not None or m.c >= HL_SLOTS:
                        act.wait_ge(s_used, (m + (1 - HL_SLOTS)).v)
                    nc.scalar.activation(w_hi[:, m.c % HL_SLOTS], raw[:, q.c % RAW_SLOTS],
                                                 ACT.Copy).then_inc(own.up(s_hi), 1)

            def round_tiles(out, src, ready, bias=None):
                act.wait_ge(s_tmp, ready)
                if bias is None:
                    ins = nc.scalar.activation(out, src, ACT.Copy)
                else:
                    ins = nc.scalar.activation(out, src, ACT.Identity, bias=bias)
                ins.then_inc(own.up(s_rnd), 1)

            def rsqrt(out, src, done, scale=1.0, power=0.0):
                nc.scalar.activation(out, src, ACT.Ln, bias=eps, scale=scale).then_inc(own.up(s_act), 1)
                act.wait_ge(*own.last())
                nc.scalar.activation(out, out, ACT.Exp, bias=power, scale=-0.5).then_inc(own.up(done), 1)

            act.wait_ge(s_vec, 16)
            nc.scalar.activation(silu_c[:], vecs[:, V_C:V_C + KT], ACT.Silu).then_inc(own.up(s_silu_c), 1)
            act.wait_ge(s_x, 16)
            act.wait_ge(s_eps, 2)
            for j, t in enumerate((t0, t1, t2, t1)):
                if j == 3:
                    act.wait_ge(s_dve, 1)
                nc.scalar.activation(t[:, 0:4 * T], wide(xres, 4 * j), ACT.Square).then_inc(own.up(s_sq), 1)
            act.wait_ge(s_stat, 1)
            rsqrt(r1[:], misc[:, 0:T], s_root, scale=1.0 / D)
            hi_parts(Num(0), 2)
            for j in range(4):
                for m in range(GM):
                    kt = GM * j + m
                    round_tiles(a_hi[:, kt], tiles(t2)[:, m], kt + 1, bias=modv[:, kt:kt + 1])
                hi_parts(Num(2 + 2 * j), 2)
            hi_parts(Num(10), AHEAD - 10)

            for j in range(4):
                act.wait_ge(s_used, (2 * j + 1) * SLABS)
                if j == 0:
                    act.wait_ge(s_pads, 1)
                else:
                    act.wait_ge(s_opnd, O_H + j)
                nc.scalar.activation(tiles(t0, 4, UW)[:, :, PAD:PAD + T], tiles(acc[:, 0]), ACT.Copy).then_inc(own.up(s_act_read), 1)
                hi_parts(Num(AHEAD + 16 * j), 5)
                round_tiles(wide(b_hi, 4 * j), (t2, t1)[j % 2][:, 0:4 * T], KT + 1 + j)
                hi_parts(Num(AHEAD + 16 * j + 5), 3)
                act.wait_ge(s_used, (2 * j + 2) * SLABS)
                nc.scalar.activation(wide(vo, 4 * j), acc[:, 1], ACT.Silu).then_inc(own.up(s_act_read), 1)
                if j < 3:
                    hi_parts(Num(AHEAD + 16 * j + 8), 8)
            hi_parts(Num(N_GRP + 7), 2)
            for j in range(4):
                round_tiles(wide(a_hi, 4 * j), (t1, t2)[j % 2][:, 0:4 * T], O_POOLED + 1 + j)
                hi_parts(Num(N_GRP + 9 + 2 * j), 2)
            hi_parts(Num(N_WOUT + 9), 6)

            for j in range(4):
                act.wait_ge(s_x1, j + 1)
                if j >= 2:
                    act.wait_ge(s_sums, 2 * j - 1)
                plain, weighed = (t3, t4) if j == 0 else (t0, t1)
                nc.scalar.activation(plain[:, 0:4 * T], wide(xres, 4 * j), ACT.Square).then_inc(own.up(s_sq), 1)
                for m in range(GM):
                    nc.scalar.activation(tiles(weighed)[:, m], xres[:, 4 * j + m], ACT.Square,
                                                 scale=vecs[:, V_FG + 4 * j + m:V_FG + 4 * j + m + 1]).then_inc(own.up(s_sq), 1)
                if j == 3:
                    act.wait_ge(s_stat, 2)
                    rsqrt(r1[:], misc[:, 0:T], s_root, scale=1.0 / D)
                    act.wait_ge(s_var2, 1)
                    rsqrt(r2[:], r2[:], s_root, scale=1.0 / D)
                    for kt in range(KT):
                        round_tiles(b_hi[:, kt], tiles(t2)[:, kt % 4], O_Z + kt + 1)
                hi_parts(slab_of(Num(G_WOUT + j)) + AHEAD, SLABS)

            act.wait_ge(s_ab, 16)
            nc.scalar.activation(ab_hi[:], ab_raw[:], ACT.Copy).then_inc(own.up(s_ab_hi), 1)
            act.wait_ge(s_ab_dve, 3)
            nc.scalar.activation(ab_t[:, 2], ab_t[:, 1], ACT.Exp).then_inc(own.up(s_ab_act), 1)
            nc.scalar.activation(ab_t[:, 3].rearrange("p (a h) -> p a h", a=2),
                                         misc[:, 1536:1600].rearrange("p (a h) -> p a h", a=2)[:, :, HEADS:],
                                         ACT.Exp, scale=-1.0).then_inc(own.up(s_ab_act), 1)
            nc.scalar.activation(ab_t[:, 4, 0:HEADS], vecs[:, V_ALOG:V_ALOG + HEADS], ACT.Exp).then_inc(own.up(s_ab_act), 1)
            act.wait_ge(*own.last(3))
            nc.scalar.activation(ab_t[:, 2], ab_t[:, 2], ACT.Ln, bias=1.0).then_inc(own.up(s_ab_act), 1)

            def first_tap(g, par):
                act.wait_ge(s_used, slab_of(g + 1).v)
                act.wait_ge(*own.last())
                for m in range(GM):
                    col = (g + (-G_A)).times(16) + (V_CONV + 4 * m + 3)
                    nc.scalar.activation(tiles(t0)[:, m], acc[:, par, m * T:(m + 1) * T], ACT.Copy,
                                                 scale=vecs[:, bass.ds(col.v, 1)]).then_inc(own.up(s_tap), 1)

            def norm_inputs(g):
                act.wait_ge(s_free, (g + 1).v)
                nc.scalar.activation(t1[:, 0:4 * T], t0[:, 0:4 * T], ACT.Silu).then_inc(own.up(s_act), 1)
                act.wait_ge(*own.last())
                nc.scalar.activation(t2[:, 0:4 * T], t1[:, 0:4 * T], ACT.Square).then_inc(own.up(s_sq2), 1)

            with act.Fori(0, 4) as i:
                own.enter(i, {s_tap: 8, s_act: 4, s_sq2: 2, s_rinv: 2, s_e: 1, s_hi: 16})
                for k, power in ((0, log_q), (1, 0.0)):
                    g = Num(G_A + k, i, 2)
                    n = slab_of(g) + AHEAD
                    first_tap(g, k)
                    hi_parts(n, 2)
                    norm_inputs(g)
                    hi_parts(n + 2, 2)
                    act.wait_ge(s_nrm, Num(1 + k, i, 2).v)
                    rsqrt(t3[:], misc[:, 0:1024], s_rinv, power=power)
                    hi_parts(n + 4, 2)
                    if k == 0:
                        act.wait_ge(s_dm, Num(1, i, 1).v)
                        nc.scalar.activation(dec_t[:], misc[:, 0:PAIRS], ACT.Exp).then_inc(own.up(s_e), 1)
                    hi_parts(n + 6, 2)
                own.leave(4)

            def solve_copies(j, step):
                out = {0: (t3[:], misc[:, 0:1024]),
                       4: (vo[:, BATCH * j:BATCH * (j + 1), 0:P],
                           misc[:, 0:512].rearrange("p (h t) -> p h t", h=BATCH)),
                       6: (vo[:, BATCH * j:BATCH * (j + 1), P:T],
                           misc[:, 0:512].rearrange("p (h t) -> p h t", h=BATCH)),
                       7: (wide(vo, BATCH * j), misc[:, 0:1024])}
                if step == 2:
                    act.wait_ge(s_solve_pe, 8 * j + 3)
                    nc.scalar.activation(t3[:], misc[:, 0:1024], ACT.Copy).then_inc(own.up(s_solve_act), 1)
                    nc.scalar.activation(wide(vo, BATCH * j), misc[:, 1024:2048], ACT.Copy).then_inc(own.up(s_solve_act), 1)
                elif step in out:
                    act.wait_ge(s_solve_pe, 8 * j + step + 1)
                    nc.scalar.activation(*out[step], ACT.Copy).then_inc(own.up(s_solve_act), 1)

            for g in range(G_A + 8, G_AOUT):
                n = slab_of(Num(g)) + AHEAD
                j = g - G_A - 12
                act.wait_ge(*own.last())
                if j < 0:
                    first_tap(Num(g), g % 2)
                else:
                    nc.scalar.activation(t4[:], wide(vo, BATCH * j), ACT.Square).then_inc(own.up(s_sq2), 1)
                for k in range(8):
                    if j < 0 and k == 1:
                        act.wait_ge(s_free, g + 1)
                        nc.scalar.activation(wide(vo, 4 * (g - G_A - 8)), t0[:, 0:4 * T], ACT.Silu).then_inc(own.up(s_vt), 1)
                    if g >= G_A + 11 and g < G_AOUT - 1 and k:
                        solve_copies(j + 1, k - 1)
                    last = g == G_AOUT - 1
                    if j >= 0 and k == (1 if last else 5):
                        act.wait_ge(s_nrm, 9 + j)
                        rsqrt(t4[:], misc[:, 1024:2048], s_rinv, scale=1.0 / P)
                    if j >= 0 and k == (2 if last else 6):
                        act.wait_ge(s_on, j + 1)
                        act.wait_ge(s_used, slab_of(Num(g + 1)).c)
                        nc.scalar.activation(t4[:], acc[:, g % 2], ACT.Silu).then_inc(own.up(s_zs), 1)
                    if j >= 0 and k == (3 if last else 7):
                        round_tiles(wide(a_hi, 4 * j), wide(vo, 4 * j), O_A + 1 + j)
                    hi_parts(n + k, 1)
                if g >= G_A + 11 and g < G_AOUT - 1:
                    solve_copies(j + 1, 7)

            for j in range(4):
                act.wait_ge(s_x1, 4 + j + 1)
                if j >= 2:
                    act.wait_ge(s_sums, 7 + j - 1)
                act.wait_ge(*own.last())
                nc.scalar.activation((t3 if j == 0 else t0)[:, 0:4 * T], wide(xres, 4 * j), ACT.Square).then_inc(own.up(s_sq), 1)
                if j == 3:
                    act.wait_ge(s_stat, 4)
                    rsqrt(r1[:], misc[:, 0:T], s_root, scale=1.0 / D)
                    for kt in range(KT):
                        round_tiles(b_hi[:, kt], tiles(t2)[:, kt % 4], O_AO + kt + 1)
                hi_parts(slab_of(Num(G_AOUT + j)) + AHEAD, SLABS)

            with act.Fori(0, 4) as i:
                own.enter(i, {s_act: 11, s_sq2: 2, s_rinv: 2, s_vn: 1, s_prob: 1, s_ptc_act: 1, s_zb: 1, s_rnd: 1,
                              s_hi: 32})
                for k, power in ((0, log_q), (1, 0.0)):
                    g = Num(G_B + k, i, 4)
                    n = slab_of(g) + AHEAD
                    if k:
                        act.wait_ge(s_bn, Num(1, i, 2).v)
                    else:
                        act.wait_ge(s_opnd, Num(O_B, i, 1).v)
                    act.wait_ge(s_used, slab_of(g + 1).v)
                    nc.scalar.activation(t0[:, 0:4 * T], acc[:, k], ACT.Copy).then_inc(own.up(s_act), 1)
                    nc.scalar.activation(t1[:, 0:4 * T], acc[:, k], ACT.Square).then_inc(own.up(s_sq2), 1)
                    hi_parts(n, 4)
                    act.wait_ge(s_nrm, Num(13 + k, i, 2).v)
                    rsqrt(t3[:], misc[:, 0:1024], s_rinv, scale=1.0 / P, power=power)
                    hi_parts(n + 4, 4)
                g = Num(G_B + 2, i, 4)
                n = slab_of(g) + AHEAD
                act.wait_ge(s_used, slab_of(g + 1).v)
                nc.scalar.activation(v_n[:].rearrange("p a c -> p (a c)"), acc[:, 0], ACT.Copy).then_inc(own.up(s_vn), 1)
                hi_parts(n, 2)
                act.wait_ge(s_max, Num(1, i, 1).v)
                for half, k, w in halves_of_pairs():
                    for h in range(BATCH):
                        at_ = k + h * w
                        last = (half, h) == (0, BATCH - 1)
                        nc.scalar.activation(p_t[:, at_:at_ + w], misc[:, at_:at_ + w], ACT.Exp,
                                                     bias=row_max[:, half, h:h + 1],
                                                     accum_out=row_sum[:, half, h:h + 1]).then_inc(own.up(s_prob if last else s_act), 1)
                hi_parts(n + 2, 4)
                act.wait_ge(s_pt, Num(1, i, 1).v)
                nc.scalar.activation(p_tt[:, 0:BATCH * T], misc[:, 0:BATCH * T], ACT.Copy).then_inc(own.up(s_ptc_act), 1)
                hi_parts(n + 6, 2)
                g = g + 1
                act.wait_ge(s_used, slab_of(g + 1).v)
                nc.scalar.activation(t1[:, 0:4 * T], acc[:, 1], ACT.Silu).then_inc(own.up(s_zb), 1)
                hi_parts(slab_of(g) + AHEAD, 2)
                act.wait_ge(s_tmp, Num(O_B + 1, i, 1).v)
                nc.scalar.activation(a_hi[:, bass.ds(i * 4, 4)].rearrange("p k t -> p (k t)"),
                                             t1[:, 0:4 * T], ACT.Copy).then_inc(own.up(s_rnd), 1)
                hi_parts(slab_of(g) + (AHEAD + 2), 6)
                own.leave(4)
            for j in range(4):
                hi_parts(slab_of(Num(G_BOUT + j)) + AHEAD, SLABS)

        @block.vector
        def _(dve):
            own = Own(s_lo)

            def add_gate(k):
                q = 3 * k + 2
                dve.wait_ge(s_raw[q % RAW_SLOTS], 16 * (q // RAW_SLOTS + 1))
                half = mod_acc[:, k % 2 * (D // 2):(k % 2 + 1) * (D // 2)]
                if k >= 2:
                    dve.wait_ge(s_gate, k - 1)
                    ins = nc.vector.scalar_tensor_tensor(out=half, in0=raw[:, q % RAW_SLOTS],
                                                         scalar=silu_c[:, k // 2:k // 2 + 1], in1=half,
                                                         op0=ALU.mult, op1=ALU.add)
                else:
                    dve.wait_ge(s_mod_sum, 5)
                    ins = nc.vector.tensor_scalar(half, raw[:, q % RAW_SLOTS], silu_c[:, 0:1], None, ALU.mult)
                ins.then_inc(own.up(s_gate), 1)

            def lo_parts(n, count):
                for k in range(count):
                    m = n + k
                    if m.var is None and m.c >= N_SLABS:
                        return
                    if m.var is None and m.c < N_GRP and m.c % 2 == 0 and m.c:
                        add_gate(m.c // 2 - 1)
                    if m.var is None and m.c == N_GRP:
                        add_gate(GATES - 1)
                    q = stream_of(m)
                    slot = m.c % HL_SLOTS
                    dve.wait_ge(s_hi, (m + 1).v)
                    nc.vector.tensor_tensor(w_lo[:, slot], raw[:, q.c % RAW_SLOTS],
                                                    w_hi[:, slot].bitcast(F32), ALU.subtract).then_inc(own.up(s_lo), 1)

            def lo_tiles(out_lo, src, hi, rounded, bias=None):
                dve.wait_ge(s_rnd, rounded)
                if bias is None:
                    ins = nc.vector.tensor_tensor(out_lo, src, hi.bitcast(F32), ALU.subtract)
                else:
                    ins = nc.vector.scalar_tensor_tensor(out=out_lo, in0=src, scalar=bias, in1=hi.bitcast(F32),
                                                         op0=ALU.add, op1=ALU.subtract)
                ins.then_inc(own.up(s_opnd), 1)

            def add(out, in0, in1, op=ALU.add, done=None):
                nc.vector.tensor_tensor(out, in0, in1, op).then_inc(own.up(done or s_dve), 1)

            def scaled(out, src, scalar, row, done=None):
                nc.vector.scalar_tensor_tensor(out=out, in0=src, scalar=scalar, in1=row,
                                                       op0=ALU.mult, op1=ALU.mult).then_inc(own.up(done or s_dve), 1)

            dve.wait_ge(s_silu_c, 1)
            for i in range(2 * KT):
                dve.wait_ge(s_mod[i % MOD_SLOTS], 16 * (i // MOD_SLOTS + 1))
                if i % KT == 0:
                    if i:
                        dve.wait_ge(s_mod_sum, 1)
                        add(modv[:, 0:KT], misc[:, 0:KT], vecs[:, V_BMOD:V_BMOD + KT], done=s_shift)
                    ins = nc.vector.tensor_scalar(mod_acc[:], mod_ring[:, i % MOD_SLOTS], silu_c[:, 0:1], None,
                                                  ALU.mult)
                else:
                    dve.wait_ge(s_mod_used, i)
                    ins = nc.vector.scalar_tensor_tensor(out=mod_acc[:], in0=mod_ring[:, i % MOD_SLOTS],
                                                         scalar=silu_c[:, i % KT:i % KT + 1], in1=mod_acc[:],
                                                         op0=ALU.mult, op1=ALU.add)
                ins.then_inc(own.up(s_mod_used), 1)
                if i == 3:
                    for k, t in enumerate((t1, t2, t1)):
                        dve.wait_ge(s_sq, k + 2)
                        if k:
                            dve.wait_ge(*own.last())
                        add(t0[:, 0:4 * T], t0[:, 0:4 * T], t[:, 0:4 * T], done=s_sums if k == 2 else None)
            lo_parts(Num(0), 2)
            for j in range(4):
                cols = slice(KT + GM * j, KT + GM * (j + 1))
                col = 512 * j + GM * j
                dve.wait_ge(s_mod_sum, 2 + j)
                dve.wait_ge(*own.last())
                nc.vector.scalar_tensor_tensor(
                    out=modv[:, cols], in0=misc[:, col:col + GM], scalar=1.0,
                    in1=vecs[:, V_BMOD + cols.start:V_BMOD + cols.stop], op0=ALU.add, op1=ALU.add).then_inc(own.up(s_dve), 1)
                dve.wait_ge(*own.last())
                dve.wait_ge(s_root, 1)
                for m in range(GM):
                    kt = GM * j + m
                    scaled(tiles(t2)[:, m], xres[:, kt], modv[:, KT + kt:KT + kt + 1], r1[:], s_tmp)
                for m in range(GM):
                    kt = GM * j + m
                    lo_tiles(a_lo[:, kt], tiles(t2)[:, m], a_hi[:, kt], kt + 1, bias=modv[:, kt:kt + 1])
                lo_parts(Num(2 + 2 * j), 2)
            lo_parts(Num(10), AHEAD - 10)

            for j, w in enumerate(WINDOWS):
                dve.wait_ge(s_act_read, 2 * j + 1)
                dve.wait_ge(*own.last())
                u = tiles(t0, 4, UW)
                src, dst, other = u, tiles(t1, 4, UW), tiles(t2, 4, UW)
                reach, d = UW, 1
                while d < w:
                    reach -= d
                    add(dst[:, :, 0:reach], src[:, :, 0:reach], src[:, :, d:d + reach],
                        done=s_free if d == 1 else s_dve)
                    dve.wait_ge(*own.last())
                    src, dst, other = dst, other, dst
                    d *= 2
                sums = src[:, :, PAD - w // 2:PAD - w // 2 + T]
                own_u = u[:, :, PAD:PAD + T]
                pooled = tiles((t2, t1)[j % 2])
                nc.vector.scalar_tensor_tensor(out=pooled, in0=sums, scalar=1.0 / w, in1=own_u,
                                                       op0=ALU.mult, op1=ALU.subtract).then_inc(own.up(s_dve), 1)
                dve.wait_ge(*own.last())
                for k, (lo, ins_at) in enumerate(((0, 0), (T - PAD, PAD))):
                    edge = pooled[:, :, lo:lo + PAD]
                    share = vecs[:, V_EDGE + 2 * PAD * j + ins_at:V_EDGE + 2 * PAD * j + ins_at + PAD]
                    add(edge, sums[:, :, lo:lo + PAD], share.unsqueeze(1).to_broadcast([P, 4, PAD]), ALU.mult)
                    dve.wait_ge(*own.last())
                    add(edge, edge, own_u[:, :, lo:lo + PAD], ALU.subtract, done=s_tmp if k else None)
                lo_parts(Num(AHEAD + 16 * j), 5)
                lo_tiles(wide(b_lo, 4 * j), (t2, t1)[j % 2][:, 0:4 * T], wide(b_hi, 4 * j), KT + 1 + j)
                lo_parts(Num(AHEAD + 16 * j + 5), 3)
                dve.wait_ge(s_act_read, 2 * j + 2)
                dve.sem_inc(own.also(s_free), 1)
                if j < 3:
                    lo_parts(Num(AHEAD + 16 * j + 8), 8)
            lo_parts(Num(N_GRP + 7), 2)
            dve.wait_ge(s_mod_sum, 6)
            add(modv[:, 2 * KT:3 * KT], misc[:, 0:KT],
                vecs[:, V_BMOD + 2 * KT:V_BMOD + 3 * KT])
            for j in range(4):
                z = (t1, t2)[j % 2]
                dve.wait_ge(s_used, N_GRP + GRP_SLABS * (j + 1))
                for m in range(GM):
                    scaled(tiles(z)[:, m], acc[:, j % 2, m * T:(m + 1) * T],
                           vecs[:, V_PSC + 4 * j + m:V_PSC + 4 * j + m + 1], vo[:, 4 * j + m],
                           done=s_tmp if m == 3 else None)
                lo_tiles(wide(a_lo, 4 * j), z[:, 0:4 * T], wide(a_hi, 4 * j), O_POOLED + 1 + j)
                dve.sem_inc(own.also(s_free), 1)
                lo_parts(Num(N_GRP + 9 + 2 * j), 2)
            lo_parts(Num(N_WOUT + 9), 6)

            for j in range(4):
                dve.wait_ge(s_used, slab_of(Num(G_WOUT + j + 1)).c)
                dve.wait_ge(*own.last())
                for m in range(GM):
                    kt = 4 * j + m
                    nc.vector.scalar_tensor_tensor(
                        out=xres[:, kt], in0=acc[:, j % 2, m * T:(m + 1) * T],
                        scalar=modv[:, 2 * KT + kt:2 * KT + kt + 1], in1=xres[:, kt],
                        op0=ALU.mult, op1=ALU.add).then_inc(own.up(s_x1 if m == 3 else s_dve), 1)
                dve.sem_inc(own.also(s_free), 1)
                if j:
                    dve.wait_ge(s_sq, 4 + 5 * j + 1)
                    add(t3[:], t3[:], t0[:, 0:4 * T], done=s_sums)
                    dve.wait_ge(s_sq, 4 + 5 * j + 5)
                    add(t4[:], t4[:], t1[:, 0:4 * T], done=s_sums)
                if j == 3:
                    dve.wait_ge(s_root, 2)
                    dve.wait_ge(s_stat, 3)
                    add(r2[:], misc[:, 512:512 + T], r1[:], ALU.mult)
                    dve.wait_ge(*own.last())
                    add(r2[:], r2[:], r1[:], ALU.mult, done=s_var2)
                    dve.wait_ge(s_root, 3)
                    for q in range(4):
                        for m in range(GM):
                            kt = 4 * q + m
                            scaled(xres[:, kt], xres[:, kt], vecs[:, V_FG + kt:V_FG + kt + 1], r1[:])
                        for m in range(GM):
                            kt = 4 * q + m
                            dve.wait_ge(*own.last(GM))
                            scaled(tiles(t2)[:, m], xres[:, kt], vecs[:, V_NW0 + kt:V_NW0 + kt + 1], r2[:], s_tmp)
                        for m in range(GM):
                            kt = 4 * q + m
                            lo_tiles(b_lo[:, kt], tiles(t2)[:, m], b_hi[:, kt], O_Z + kt + 1)
                lo_parts(slab_of(Num(G_WOUT + j)) + AHEAD, SLABS)

            dve.wait_ge(s_ab_hi, 1)
            nc.vector.tensor_tensor(ab_lo[:], ab_raw[:], ab_hi[:].bitcast(F32), ALU.subtract).then_inc(own.up(s_ab_lo), 1)
            dve.wait_ge(s_ab_mm, 1)
            ab = misc[:, 1536:1600].rearrange("p (a h) -> p a h", a=2)
            halves = [ab_t[:, k].rearrange("p (a h) -> p a h", a=2) for k in range(5)]
            dtb = vecs[:, V_DTB:V_DTB + HEADS].unsqueeze(1).to_broadcast([P, 2, HEADS])
            add(halves[0], ab[:, :, 0:HEADS], dtb, done=s_ab_dve)
            dve.wait_ge(*own.last())
            nc.vector.tensor_scalar(ab_t[:, 1], ab_t[:, 0], -1.0, None, ALU.mult).then_inc(own.up(s_ab_dve), 1)
            dve.wait_ge(*own.last())
            add(ab_t[:, 1], ab_t[:, 0], ab_t[:, 1], ALU.min, done=s_ab_dve)
            nc.vector.tensor_scalar(ab_t[:, 0], ab_t[:, 0], 0.0, None, ALU.max).then_inc(own.up(s_dve), 1)
            dve.wait_ge(s_ab_act, 2)
            nc.vector.tensor_scalar(ab_t[:, 3], ab_t[:, 3], 1.0, None, ALU.add).then_inc(own.up(s_dve), 1)
            dve.wait_ge(*own.last())
            nc.vector.reciprocal(beta[:], ab_t[:, 3]).then_inc(own.up(s_dve), 1)
            dve.wait_ge(s_ab_act, 4)
            add(ab_t[:, 0], ab_t[:, 0], ab_t[:, 2], done=s_ab_dve)
            dve.wait_ge(*own.last())
            nc.vector.scalar_tensor_tensor(
                out=decay[:].rearrange("p (a h) -> p a h", a=2), in0=halves[0], scalar=-1.0,
                in1=ab_t[:, 4, 0:HEADS].unsqueeze(1).to_broadcast([P, 2, HEADS]), op0=ALU.mult, op1=ALU.mult).then_inc(own.up(s_ab_dve), 1)

            def other_taps(g, par):
                col = (g + (-G_A)).times(16) + V_CONV
                dve.wait_ge(*own.last())
                nc.vector.tensor_copy(conv_now[:], vecs[:, bass.ds(col.v, 16)]).then_inc(own.up(s_dve), 1)
                dve.wait_ge(*own.last())
                dve.wait_ge(s_tap, (g + (1 - G_A)).times(4).v)
                for d in range(1, 4):
                    for m in range(GM):
                        if d > 1:
                            dve.wait_ge(*own.last(GM))
                        out = tiles(t0)[:, m, d:T]
                        src = acc[:, par, m * T:(m + 1) * T - d]
                        ins = nc.vector.scalar_tensor_tensor(out=out, in0=src,
                                                             scalar=conv_now[:, 4 * m + 3 - d:4 * m + 4 - d],
                                                             in1=out, op0=ALU.mult, op1=ALU.add)
                        ins.then_inc(own.up(s_free if (d, m) == (3, GM - 1) else s_dve), 1)

            def pair_products(out, done):
                for h in range(BATCH):
                    for half, k, w in ((0, h * T, T), (1, BATCH * T + h * P, P)):
                        last = (h, half) == (BATCH - 1, 1)
                        scaled(out[:, k:k + w], misc[:, k:k + w], beta_now[:, half, h:h + 1], dec_t[:, k:k + w],
                               done=done if last else None)

            with dve.Fori(0, 4) as i:
                own.enter(i, {s_dve: 39, s_free: 2, s_qkn: 2, s_l: 1, s_a: 1, s_lo: 16})
                for k, out in ((0, q_n), (1, k_n)):
                    g = Num(G_A + k, i, 2)
                    n = slab_of(g) + AHEAD
                    other_taps(g, k)
                    lo_parts(n, 5)
                    dve.wait_ge(s_rinv, Num(1 + k, i, 2).v)
                    add(out[:], t1[:, 0:4 * T], t3[:], ALU.mult, done=s_qkn)
                    lo_parts(n + 5, 1)
                    if k:
                        nc.vector.tensor_copy(
                            beta_now[:], beta[:].rearrange("p (a h) -> p a h", a=2)[:, :, bass.ds(i * BATCH, BATCH)]).then_inc(own.up(s_dve), 1)
                        dve.wait_ge(*own.last())
                        dve.wait_ge(s_em, Num(2, i, 2).v)
                        dve.wait_ge(s_kk, Num(1, i, 1).v)
                        pair_products(l_t, s_l)
                    lo_parts(n + 6, 1)
                    if k:
                        dve.wait_ge(s_qk, Num(1, i, 1).v)
                        pair_products(a_t, s_a)
                    lo_parts(n + 7, 1)
                own.leave(4)

            def invert(s):
                below = 31 - s
                tmp = prod[:, 0:below * (s + 1)].rearrange("p (t c) -> p t c", t=below)
                row = inv[:, s, 0:s + 1].unsqueeze(1).to_broadcast([P, below, s + 1])
                col = blk[:, s, s + 1:32].unsqueeze(2).to_broadcast([P, below, s + 1])
                dve.wait_ge(*own.last())
                add(tmp, col, row, ALU.mult)
                dve.wait_ge(*own.last())
                add(inv[:, s + 1:32, 0:s + 1], inv[:, s + 1:32, 0:s + 1], tmp, ALU.subtract)

            def solve_updates(j, step):
                if step in (1, 3):
                    dve.wait_ge(s_solve_pe, 8 * j + step + 1)
                    y = t0[:, 0:1024]
                    add(y, y, misc[:, 1024:2048], ALU.subtract, done=s_solve_dve if step == 3 else None)
                    if step == 1:
                        x = t1[:, 0:1024]
                        add(x, x, misc[:, 0:1024], ALU.subtract, done=s_solve_dve)
                if step == 5:
                    dve.wait_ge(s_solve_pe, 8 * j + 6)
                    v = vo[:, BATCH * j:BATCH * (j + 1), P:T]
                    add(v, v, misc[:, 512:1024].rearrange("p (h t) -> p h t", h=BATCH), ALU.subtract,
                        done=s_solve_dve)

            rows = {G_A + 8: (3, range(0, 8)), G_A + 9: (0, range(8, 20)), G_A + 10: (0, range(20, 31))}
            for g in range(G_A + 8, G_AOUT):
                n = slab_of(Num(g)) + AHEAD
                j = g - G_A - 12
                dve.wait_ge(*own.last())
                if j < 0:
                    other_taps(Num(g), g % 2)
                for k in range(8):
                    if g >= G_A + 11 and g < G_AOUT - 1 and k:
                        solve_updates(j + 1, k - 1)
                    if g in rows:
                        k0, which = rows[g]
                        if g == G_A + 8 and k == k0:
                            nc.vector.memset(inv[:], 0.0).then_inc(own.up(s_dve), 1)
                            dve.wait_ge(*own.last())
                            flat = inv[:].rearrange("p a b -> p (a b)")
                            nc.vector.memset(flat[:, 0:1024:33], 1.0).then_inc(own.up(s_dve), 1)
                            dve.wait_ge(s_blk, 16 * 8)
                        if k >= k0:
                            part = -(-len(which) // (8 - k0))
                            for r in which[(k - k0) * part:(k - k0 + 1) * part]:
                                invert(r)
                        if g == G_A + 10 and k == 7:
                            dve.wait_ge(*own.last())
                            nc.vector.tensor_copy(inv_t[:], inv[:].rearrange("p t s -> p s t")).then_inc(own.up(s_inv), 1)
                    last = g == G_AOUT - 1
                    o = wide(vo, 4 * j) if j >= 0 else None
                    if j >= 0 and k == (1 if last else 5):
                        dve.wait_ge(s_rinv, 9 + j)
                        scaled(o, o, vecs[:, V_ONW:V_ONW + 1], t4[:], done=s_on)
                    if j >= 0 and k == (2 if last else 6):
                        dve.wait_ge(*own.last())
                        dve.wait_ge(s_zs, j + 1)
                        add(o, o, t4[:], ALU.mult, done=s_tmp)
                        dve.sem_inc(own.also(s_free), 1)
                    if j >= 0 and k == (3 if last else 7):
                        lo_tiles(wide(a_lo, 4 * j), o, wide(a_hi, 4 * j), O_A + 1 + j)
                    lo_parts(n + k, 1)

            dve.wait_ge(s_xb, 16)
            for j in range(4):
                dve.wait_ge(s_used, slab_of(Num(G_AOUT + j + 1)).c)
                add(wide(xres, 4 * j), acc[:, j % 2], wide(xres, 4 * j), done=s_x1)
                dve.sem_inc(own.also(s_free), 1)
                if j:
                    dve.wait_ge(s_sq, 24 + j + 1)
                    add(t3[:], t3[:], t0[:, 0:4 * T], done=s_sums)
                if j == 3:
                    dve.wait_ge(s_root, 4)
                    for q in range(4):
                        dve.wait_ge(*own.last())
                        for m in range(GM):
                            kt = 4 * q + m
                            scaled(tiles(t2)[:, m], xres[:, kt], vecs[:, V_NW1 + kt:V_NW1 + kt + 1], r1[:], s_tmp)
                        for m in range(GM):
                            kt = 4 * q + m
                            lo_tiles(b_lo[:, kt], tiles(t2)[:, m], b_hi[:, kt], O_AO + kt + 1)
                lo_parts(slab_of(Num(G_AOUT + j)) + AHEAD, SLABS)

            def by_head(t, k, w):
                return t[:, k:k + BATCH * w].rearrange("p (h s) -> p h s", h=BATCH)

            with dve.Fori(0, 4) as i:
                own.enter(i, {s_free: 4, s_bn: 2, s_max: 1, s_pn: 1, s_ptc_dve: 1, s_tmp: 1, s_opnd: 1,
                              s_dve: 5, s_lo: 32})
                for k, (out, w) in enumerate(((t2, V_QNW), (t0, V_KNW))):
                    n = slab_of(Num(G_B + k, i, 4)) + AHEAD
                    dve.wait_ge(s_sq2, Num(13 + k, i, 2).v)
                    dve.sem_inc(own.also(s_free), 1)
                    lo_parts(n, 5)
                    dve.wait_ge(s_rinv, Num(13 + k, i, 2).v)
                    scaled(out[:, 0:4 * T], t0[:, 0:4 * T], vecs[:, w:w + 1], t3[:], done=s_bn)
                    lo_parts(n + 5, 2)
                    if k:
                        dve.wait_ge(s_score, Num(1, i, 1).v)
                        for half, at_, w in halves_of_pairs():
                            nc.vector.memset(by_head(misc, at_, w)[0:CHUNK, :, w - CHUNK:w], MASKED).then_inc(own.up(s_dve), 1)
                        dve.wait_ge(*own.last())
                        for half, at_, w in halves_of_pairs():
                            nc.vector.tensor_reduce(row_max[:, half], by_head(misc, at_, w),
                                                            mybir.AxisListType.X, ALU.max, negate=True).then_inc(own.up(s_dve if half else s_max), 1)
                    lo_parts(n + 7, 1)
                n = slab_of(Num(G_B + 2, i, 4)) + AHEAD
                dve.wait_ge(s_vn, Num(1, i, 1).v)
                dve.sem_inc(own.also(s_free), 1)
                lo_parts(n, 3)
                dve.wait_ge(s_prob, Num(1, i, 1).v)
                nc.vector.reciprocal(row_sum[:], row_sum[:]).then_inc(own.up(s_dve), 1)
                dve.wait_ge(*own.last())
                for half, at_, w in halves_of_pairs():
                    p = by_head(p_t, at_, w)
                    add(p, p, row_sum[:, half].unsqueeze(2).to_broadcast([P, BATCH, w]), ALU.mult,
                        done=None if half else s_pn)
                lo_parts(n + 3, 3)
                dve.wait_ge(s_pt, Num(1, i, 1).v)
                nc.vector.tensor_copy(p_tt[:, BATCH * T:PAIRS], misc[:, BATCH * T:PAIRS]).then_inc(own.up(s_ptc_dve), 1)
                lo_parts(n + 6, 2)
                n = n + SLABS
                dve.wait_ge(s_zb, Num(1, i, 1).v)
                dve.wait_ge(s_pv, Num(1, i, 1).v)
                add(t1[:, 0:4 * T], t1[:, 0:4 * T], misc[:, 0:4 * T], ALU.mult, done=s_tmp)
                dve.sem_inc(own.also(s_free), 1)
                lo_parts(n, 2)
                dve.wait_ge(s_rnd, Num(O_B + 1, i, 1).v)
                nc.vector.tensor_tensor(
                    a_lo[:, bass.ds(i * 4, 4)].rearrange("p k t -> p (k t)"), t1[:, 0:4 * T],
                    a_hi[:, bass.ds(i * 4, 4)].rearrange("p k t -> p (k t)").bitcast(F32), ALU.subtract).then_inc(own.up(s_opnd), 1)
                lo_parts(n + 2, 6)
                own.leave(4)
            for j in range(4):
                dve.wait_ge(s_used, slab_of(Num(G_BOUT + j + 1)).c)
                add(wide(vo, 4 * j), acc[:, j % 2], wide(xres, 4 * j), done=s_y)
                dve.sem_inc(own.also(s_free), 1)
                lo_parts(slab_of(Num(G_BOUT + j)) + AHEAD, SLABS)



def slabs(m, groups):
    k = m.shape[0]
    cols = np.stack([m[:, c:c + GC] for c in groups])
    s = cols.reshape(len(groups), k // (SLAB_K * P), SLAB_K, P, GC).transpose(0, 1, 3, 2, 4)
    return s.reshape(-1, P, SLAB_K * GC)


def channels(v):
    return v.reshape(-1, P).T


def build_stream(i):
    w_in = i["pool_w_in"][0]
    ug = slabs(w_in, [c for j in range(4) for c in (GC * j, D + GC * j)])
    gate = i["w_mod"][0][:, 2 * D:].reshape(KT, P, 2, D // 2).transpose(0, 2, 1, 3).reshape(GATES, 1, P, D // 2)
    ug = np.concatenate([ug.reshape(GATES, 2, P, SLAB_K * GC), gate], axis=1).reshape(-1, P, SLAB_K * GC)
    grp = np.concatenate([slabs(i["pool_w_grp"][0, j], [0]) for j in range(4)])
    quarters = [GC * j for j in range(4)]
    a = i["a_w_in_2"][0]
    order_a = [c for j in range(4) for c in (GC * j, D + GC * j)]
    order_a += [2 * D + GC * j for j in range(4)] + [3 * D + GC * j for j in range(4)]
    order_b = [k * D + GC * j for j in range(4) for k in range(4)]
    return np.concatenate([ug, grp, slabs(i["pool_w_out"][0], quarters), slabs(a, order_a),
                           slabs(i["a_w_out_2"][0], quarters), slabs(i["b_w_in_2"][0], order_b),
                           slabs(i["b_w_out_2"][0], quarters)]).reshape(-1, SLAB_K * GC), order_a


def build_vecs(i, order_a):
    conv = i["a_conv_w_2"][0]
    conv = np.stack([conv[:, c + P * m:c + P * (m + 1)] for c in order_a[:12] for m in range(GM)])
    edges = np.zeros((4, 2 * PAD), np.float32)
    for j, w in enumerate(WINDOWS):
        for k, t in enumerate([*range(PAD), *range(T - PAD, T)]):
            edges[j, k] = 1.0 / (min(t + w // 2, T) - max(t - w // 2, 0))
    rows = [i["a_a_log_2"][0], i["a_dt_bias_2"][0], edges.reshape(-1)]
    return np.concatenate([
        channels(i["c"][0]), channels(i["b_mod"][0]), channels(i["pool_scale"][0]), channels(i["final_norm_g"]),
        channels(i["norm_w_2"][0]), channels(i["norm_w_2"][1]), conv.transpose(2, 0, 1).reshape(P, -1),
        i["a_out_norm_w_2"].T, i["b_q_norm_w_2"].T, i["b_k_norm_w_2"].T,
        *[np.broadcast_to(r, (P, r.size)) for r in rows]], axis=1)


def build_consts():
    r, c = np.arange(P)[:, None], np.arange(P)[None, :]
    one = np.ones((P, P))
    half, quarter = c // 64 == r // 64, c // 32 == r // 32
    return np.concatenate([r == c, r > c, one, r <= c, one, quarter, half & ~quarter, ~half,
                           r + c == P - 1],
                          axis=1).astype(np.float32)


def kernel(**inputs):
    import concourse.bacc as bacc
    from concourse.bass_utils import run_bass_kernel_spmd

    i = {k: np.asarray(v) for k, v in inputs.items()}
    stream, order_a = build_stream(i)
    mod = i["w_mod"][0][:, :2 * D].reshape(KT, P, 2, D).transpose(2, 0, 1, 3).reshape(2 * KT, P, D)
    rel = i["b_rel_bias_2"][0]
    arrays = {
        "weights": stream,
        "mod_w": mod,
        "x_t": i["x"][0].T.reshape(KT, P, T).transpose(1, 0, 2),
        "vecs": build_vecs(i, order_a),
        "consts": build_consts(),
        "w_ab": i["a_w_in_2"][0][:, 4 * D:].reshape(KT, P, 2 * HEADS).transpose(1, 0, 2),
        "bias": rel[:, ::-1],
    }
    arrays = {k: np.ascontiguousarray(v) for k, v in arrays.items()}
    nc = bacc.Bacc("TRN2", target_bir_lowering=False, num_devices=1)
    args = [nc.dram_tensor(k, v.shape, F32, kind="ExternalInput").ap() for k, v in arrays.items()]
    out = nc.dram_tensor("out", (P, KT, T), F32, kind="ExternalOutput").ap()
    program(nc, *args, out)
    r = run_bass_kernel_spmd(nc, [arrays], core_ids=[0])
    return r.results[0]["out"].transpose(2, 1, 0).reshape(1, T, D)
```

```python
from contextlib import ExitStack

import numpy as np
import concourse.bass as bass
from concourse import mybir

F32 = mybir.dt.float32
F32R = mybir.dt.float32r
ACT = mybir.ActivationFunctionType
ALU = mybir.AluOpType

P = 128
D = 2048
T = 256
KT = D // P
GC = 512
GM = GC // P
SLAB_K = 2
SLABS = KT // SLAB_K
RAW_SLOTS = 4
HL_SLOTS = 8
AHEAD = 15
EPS = 1e-6
HEADS = 16
CHUNK = 64
BATCH = 4
WINDOWS = (2, 4, 8, 16)
PAD = 8
UW = T + 2 * PAD
REL = 2 * T + 1
MASKED = -3e38
MOD_SLOTS = 6
PAIRS = BATCH * (T + P)
GATES = 2 * KT

G_UG, G_GRP, G_WOUT, G_A, G_AOUT, G_B, G_BOUT, G_END = 0, 8, 12, 16, 32, 36, 52, 56
GRP_SLABS = GM // SLAB_K
N_GRP = 8 * SLABS
N_WOUT = N_GRP + 4 * GRP_SLABS
N_SLABS = N_WOUT + (G_END - G_WOUT) * SLABS

O_H, O_POOLED, O_Z = KT, KT + 4, KT + 8
O_A = O_Z + KT
O_AO = O_A + 4
O_B = O_AO + KT

V_C, V_BMOD, V_PSC, V_FG, V_NW0, V_NW1, V_CONV = 0, 16, 64, 80, 96, 112, 128
V_ONW, V_QNW, V_KNW, V_ALOG, V_DTB, V_EDGE, V_END = 320, 321, 322, 323, 339, 355, 419
C_ID, C_GT, C_ONE, C_UP, C_BD, C_M1, C_M2, C_END = 0, 128, 256, 384, 640, 768, 896, 1024


class Num:

    def __init__(self, c, var=None, mul=0):
        self.c, self.var, self.mul = c, var, mul

    def __add__(self, k):
        return Num(self.c + k, self.var, self.mul)

    def times(self, k):
        return Num(self.c * k, self.var, self.mul * k)

    @property
    def v(self):
        return self.c if self.var is None or self.mul == 0 else self.var * self.mul + self.c


class Own:

    def __init__(self, main):
        self.main, self.count, self.steps, self.loop_of = main, {}, [], None

    def also(self, sem):
        self.count[sem.name] = self.count.get(sem.name, Num(0)) + 1
        return sem

    def up(self, sem):
        self.also(sem)
        self.steps.append((sem, self.count[sem.name]))
        return sem

    def last(self, k=1):
        sem, n = self.steps[-k]
        return sem, n.v

    def reset(self):
        self.steps = [(self.main, self.count[self.main.name])]

    def enter(self, i, per):
        for s, k in per.items():
            self.count[s.name] = Num(self.count.get(s.name, Num(0)).c, i, k)
        self.loop_of = (dict(self.count), per)
        self.reset()

    def leave(self, times):
        was, per = self.loop_of
        rose = {n: self.count[n].c - was.get(n, Num(0)).c for n in self.count}
        told = {s.name: k for s, k in per.items()}
        assert {n: k for n, k in rose.items() if k} == told, (rose, told)
        for n in self.count:
            self.count[n] = Num(was[n].c + was[n].mul * times)
        self.reset()


def slab_of(g):
    return g.times(SLABS) + (N_WOUT - G_WOUT * SLABS)


def program(nc, weights, mod_w, x_t, vecs_d, consts_d, w_ab_d, bias_d, out_d):
    ctx = ExitStack()
    with ctx:
        top = [nc.sbuf_base + (-nc.sbuf_base) % 64]

        def at(name, shape, dtype, offset=None):
            size = int(np.prod(shape[1:])) * 4
            if offset is None:
                offset = top[0]
                top[0] += size + (-size) % 32
            return nc.alloc_sbuf_tensor_at(name, shape, dtype, offset=offset)

        def sem(name):
            return ctx.enter_context(nc.semaphore(name))

        raw = at("raw", [P, RAW_SLOTS, SLAB_K * GC], F32)
        w_hi = at("w_hi", [P, HL_SLOTS, SLAB_K * GC], F32R)
        w_lo = at("w_lo", [P, HL_SLOTS, SLAB_K * GC], F32R)
        a_at = top[0]
        a_hi = at("a_hi", [P, KT, T], F32R)
        a_lo = at("a_lo", [P, KT, T], F32R)
        b_at = top[0]
        b_hi = at("b_hi", [P, KT, T], F32R)
        b_lo = at("b_lo", [P, KT, T], F32R)
        vo_at = top[0]
        vo = at("vo", [P, KT, T], F32)
        x_at = top[0]
        xres = at("xres", [P, KT, T], F32)
        t0 = at("t0", [P, 4 * UW], F32)
        t1 = at("t1", [P, 4 * UW], F32)
        t2 = at("t2", [P, 4 * UW], F32)
        t34_at = top[0]
        t3 = at("t3", [P, 4 * T], F32)
        t4 = at("t4", [P, 4 * T], F32)
        vecs = at("vecs", [P, V_END], F32)
        consts = at("consts", [P, C_END], F32)
        r1 = at("r1", [P, T], F32)
        r2 = at("r2", [P, T], F32)
        ones_r = at("ones_r", [P, P], F32R)
        gains = at("gains", [P, KT], F32)
        silu_c = at("silu_c", [P, KT], F32)
        modv = at("modv", [P, 3 * KT], F32)
        small = at("small", [P, 4], F32)
        decay = at("decay", [P, 2 * HEADS], F32)
        beta = at("beta", [P, 2 * HEADS], F32)
        ab_t = at("ab_t", [P, 5, 2 * HEADS], F32)
        beta_now = at("beta_now", [P, 2, BATCH], F32)
        row_max = at("row_max", [P, 2, BATCH], F32)
        row_sum = at("row_sum", [P, 2, BATCH], F32)
        conv_now = at("conv_now", [P, GM * 4], F32)
        assert top[0] <= nc.sbuf_usable_end, top[0]
        mod_ring = at("mod_ring", [P, MOD_SLOTS, D], F32, b_at)
        mod_acc = at("mod_acc", [P, D], F32, t34_at)
        q_n = at("q_n", [P, 4 * T], F32, a_at)
        k_n = at("k_n", [P, 4 * T], F32, a_at + 4096)
        dec_t = at("dec_t", [P, PAIRS], F32, a_at + 8192)
        gu_t = at("gu_t", [P, PAIRS], F32, a_at + 14336)
        l_t = at("l_t", [P, PAIRS], F32, a_at + 20480)
        a_t = at("a_t", [P, PAIRS], F32, a_at + 26624)
        ab_raw = at("ab_raw", [P, KT * 2 * HEADS], F32, vo_at)
        ab_hi = at("ab_hi", [P, KT * 2 * HEADS], F32R, vo_at + 2048)
        ab_lo = at("ab_lo", [P, KT * 2 * HEADS], F32R, vo_at + 4096)
        ab_c = at("ab_c", [P, T], F32, vo_at + 6144)
        blk = at("blk", [P, 32, 32], F32, a_at)
        inv = at("inv", [P, 32, 32], F32, a_at + 4096)
        inv_t = at("inv_t", [P, 32, 32], F32, a_at + 8192)
        prod = at("prod", [P, 256], F32, a_at + 12288)
        l_x = at("l_x", [P, PAIRS], F32, x_at)
        a_x = at("a_x", [P, PAIRS], F32, x_at + 6144)
        xc = at("xc", [P, 2 * BATCH * 32], F32, x_at + 12288)
        yc = at("yc", [P, 2 * BATCH * 32], F32, x_at + 13312)
        p_t = at("p_t", [P, PAIRS], F32, vo_at)
        p_tt = at("p_tt", [P, PAIRS], F32, vo_at + 4 * PAIRS)
        sq_hi = at("sq_hi", [P, 4 * T], F32R, vo_at)
        sq_lo = at("sq_lo", [P, 4 * T], F32R, vo_at + 16 * T)
        v_n = at("v_n", [P, 2, GC], F32, vo_at + 8 * PAIRS)
        acc = ctx.enter_context(nc.psum_tensor("acc", [P, 2, 4 * T], F32))
        misc = ctx.enter_context(nc.psum_tensor("misc", [P, 2048], F32))

        ident = consts[:, C_ID:C_ID + P]
        ones = consts[:, C_ONE:C_ONE + P]
        eps = small[:, 0:1]
        log_q = small[:, 1:2]

        def tiles(t, n=4, w=T):
            return t[:, 0:n * w].rearrange("p (k t) -> p k t", k=n)

        l_d = [nc.dram_tensor(f"l{k}_d", (P, HEADS * w), F32).ap() for k, w in ((0, T), (1, P))]
        a_d = [nc.dram_tensor(f"a{k}_d", (P, HEADS * w), F32).ap() for k, w in ((0, T), (1, P))]
        inv_d = [nc.dram_tensor(f"inv{k}_d", (P, 2, HEADS, 32), F32).ap() for k in (0, 1)]
        bias_x = nc.dram_tensor("bias_x", (P, HEADS * T), F32).ap()
        x_d = nc.dram_tensor("x_d", (P, KT, T), F32).ap()

        s_raw = [sem(f"s_raw{i}") for i in range(RAW_SLOTS)]
        s_hi = sem("s_hi")
        s_lo = sem("s_lo")
        s_gate = sem("s_gate")
        s_used = sem("s_used")
        s_free = sem("s_free")
        s_opnd = sem("s_opnd")
        s_tmp = sem("s_tmp")
        s_rnd = sem("s_rnd")
        s_mod = [sem(f"s_mod{i}") for i in range(MOD_SLOTS)]
        s_mod_used = sem("s_mod_used")
        s_mod_sum = sem("s_mod_sum")
        s_vec = sem("s_vec")
        s_con = sem("s_con")
        s_x = sem("s_x")
        s_shift = sem("s_shift")
        s_silu_c = sem("s_silu_c")
        s_sq = sem("s_sq")
        s_sums = sem("s_sums")
        s_stat = sem("s_stat")
        s_root = sem("s_root")
        s_var2 = sem("s_var2")
        s_act_read = sem("s_act_read")
        s_x1 = sem("s_x1")
        s_eps = sem("s_eps")
        s_pads = sem("s_pads")
        s_dve = sem("s_dve")
        s_act = sem("s_act")
        s_outs = [sem(f"s_outs{j}") for j in range(4)]
        s_ab = sem("s_ab")
        s_ab_hi = sem("s_ab_hi")
        s_ab_lo = sem("s_ab_lo")
        s_ab_mm = sem("s_ab_mm")
        s_ab_act = sem("s_ab_act")
        s_ab_dve = sem("s_ab_dve")
        s_tap = sem("s_tap")
        s_sq2 = sem("s_sq2")
        s_nrm = sem("s_nrm")
        s_rinv = sem("s_rinv")
        s_qkn = sem("s_qkn")
        s_gu = sem("s_gu")
        s_dm = sem("s_dm")
        s_e = sem("s_e")
        s_em = sem("s_em")
        s_kk = sem("s_kk")
        s_qk = sem("s_qk")
        s_l = sem("s_l")
        s_a = sem("s_a")
        s_ld = [sem("s_ld0"), sem("s_ld1")]
        s_ad = [sem("s_ad0"), sem("s_ad1")]
        s_blk = sem("s_blk")
        s_inv = sem("s_inv")
        s_invd = sem("s_invd")
        s_xn = sem("s_xn")
        s_xd = sem("s_xd")
        s_xb = sem("s_xb")
        s_vt = sem("s_vt")
        s_lx = [sem("s_lx0"), sem("s_lx1")]
        s_ax = [sem("s_ax0"), sem("s_ax1")]
        s_cx = [sem("s_cx0"), sem("s_cx1")]
        s_dense = sem("s_dense")
        s_solve_pe = sem("s_solve_pe")
        s_solve_act = sem("s_solve_act")
        s_solve_dve = sem("s_solve_dve")
        s_on = sem("s_on")
        s_zs = sem("s_zs")

        s_ones = sem("s_ones")
        s_sqh = sem("s_sqh")
        s_sql = sem("s_sql")
        s_bx = sem("s_bx")
        s_biased = sem("s_biased")
        s_bias = sem("s_bias")
        s_bn = sem("s_bn")
        s_score = sem("s_score")
        s_max = sem("s_max")
        s_prob = sem("s_prob")
        s_pn = sem("s_pn")
        s_pt = sem("s_pt")
        s_ptc_act = sem("s_ptc_act")
        s_ptc_dve = sem("s_ptc_dve")
        s_vn = sem("s_vn")
        s_pv = sem("s_pv")
        s_zb = sem("s_zb")
        s_y = sem("s_y")

        block = ctx.enter_context(nc.Block())

        @block.sync
        def _(sp):
            sp.dma_start(vecs[:], vecs_d).then_inc(s_vec, 16)
            for i in range(2 * KT):
                if i >= MOD_SLOTS:
                    sp.wait_ge(s_mod_used, i - MOD_SLOTS + 1)
                sp.dma_start(mod_ring[:, i % MOD_SLOTS], mod_w[i]).then_inc(s_mod[i % MOD_SLOTS], 16)
                if i == 1:
                    sp.dma_start(xres[:], x_t).then_inc(s_x, 16)

            def piece(q, slot, var=None, mul=0):
                before = q - RAW_SLOTS
                if before >= 0 or var is not None:
                    if before % 3 == 2:
                        sp.wait_ge(s_gate, Num(before // 3 + 1, var, mul // 3).v)
                    else:
                        sp.wait_ge(s_lo, Num(before // 3 * 2 + before % 3 + 1, var, mul // 3 * 2).v)
                land(Num(q, var, mul), slot)

            def land(q, slot):
                sp.dma_start(raw[:, slot], weights[bass.ds(q.times(P).v, P), :]).then_inc(s_raw[slot], 16)

            for q in range(12):
                piece(q, q % RAW_SLOTS)
            with sp.Fori(1, 8) as i:
                for q in range(12):
                    piece(q, q % RAW_SLOTS, i, 12)
            for q in range(12 * 8, 12 * 8 + 4):
                piece(q, q % RAW_SLOTS)
            def slabs_between(a, b):
                with sp.Fori(a // 4, b // 4) as i:
                    for k in range(4):
                        sp.wait_ge(s_lo, Num(k - 3, i, 4).v)
                        land(Num(GATES + k, i, 4), k)

            middle = slab_of(Num(G_A + 9)).c + AHEAD + SLABS + 1
            slabs_between(N_GRP + 4, middle)
            sp.wait_ge(s_inv, 1)
            for k, tile in enumerate((inv, inv_t)):
                for half in range(2):
                    for b in range(4):
                        at_ = (half * 4 + b) * HEADS
                        dst = inv_d[k][32 * b:32 * b + 32, half].rearrange("s h t -> h s t")
                        sp.dma_start(dst, tile[at_:at_ + HEADS]).then_inc(s_invd, 16)
                    m = middle + 2 * k + half
                    sp.wait_ge(s_lo, m - RAW_SLOTS + 1)
                    land(Num(GATES + m), m % RAW_SLOTS)
            slabs_between(middle + 4, N_SLABS)
            for j in range(4):
                sp.wait_ge(s_y, j + 1)
                sp.dma_start(out_d[:, 4 * j:4 * j + 4], vo[:, 4 * j:4 * j + 4]).then_inc(s_outs[j], 16)
            for j in range(4):
                sp.wait_ge(s_outs[j], 16)

        @block.gpsimd
        def _(pool):
            pool.dma_start(consts[:], consts_d).then_inc(s_con, 16)
            pool.memset(small[:, 0:1], EPS).then_inc(s_eps, 1)
            pool.memset(small[:, 1:2], -0.5 * float(np.log(P))).then_inc(s_eps, 1)
            pool.wait_ge(s_stat, 1)
            pool.memset(t0[:], 0.0).then_inc(s_pads, 1)
            pool.wait_ge(s_opnd, O_Z)
            pool.dma_start(ab_raw[:], w_ab_d.rearrange("p k c -> p (k c)")).then_inc(s_ab, 16)

            up = consts[:, C_UP:C_UP + T]
            up_tile = up[:, 0:P].unsqueeze(1).to_broadcast([P, BATCH, P])
            pool.wait_ge(s_ab_dve, 6)
            for i in range(4):
                if i:
                    pool.wait_ge(s_dm, i)
                for h in range(BATCH):
                    for b, w, at_ in ((0, T, h * T), (1, P, BATCH * T + h * P)):
                        col = b * HEADS + BATCH * i + h
                        last = pool.tensor_scalar(gu_t[:, at_:at_ + w], up[:, 0:w], decay[:, col:col + 1], None,
                                                  ALU.mult)
                        last.then_inc(s_gu, 1)
                if i == 0:
                    pool.wait_ge(s_opnd, O_A)
                    root = r1[:].unsqueeze(1).to_broadcast([P, GM, T])
                    for k in range(2):
                        for q in range(4):
                            x = xres[:, 4 * q:4 * q + 4]
                            gain = vecs[:, V_FG + 4 * q:V_FG + 4 * q + 4].unsqueeze(2).to_broadcast([P, GM, T])
                            if k:
                                pool.wait_ge(s_xn, q + 1)
                            pool.tensor_tensor(x, x, gain if k else root, ALU.mult).then_inc(s_xn, 1)
                    pool.wait_ge(s_xn, 8)
                    pool.dma_start(x_d, xres[:]).then_inc(s_xd, 16)
                if i:
                    for k in range(2):
                        pool.wait_ge(s_ld[k], 16 * i)
                        pool.wait_ge(s_ad[k], 16 * i)
                pool.wait_ge(s_e, i + 1)
                for view in (dec_t[:, 0:BATCH * T].rearrange("p (h t) -> p h t", h=BATCH)[:, :, 0:P],
                             dec_t[:, BATCH * T:PAIRS].rearrange("p (h t) -> p h t", h=BATCH)):
                    pool.tensor_tensor(view, view, up_tile, ALU.mult).then_inc(s_em, 1)
                for tile, done, dst, sems in ((l_t, s_l, l_d, s_ld), (a_t, s_a, a_d, s_ad)):
                    pool.wait_ge(done, i + 1)
                    pool.dma_start(dst[0][:, BATCH * T * i:BATCH * T * (i + 1)], tile[:, 0:BATCH * T]
                                   ).then_inc(sems[0], 16)
                    pool.dma_start(dst[1][:, BATCH * P * i:BATCH * P * (i + 1)], tile[:, BATCH * T:PAIRS]
                                   ).then_inc(sems[1], 16)

            for k in range(2):
                pool.wait_ge(s_ld[k], 64)
            for half in range(2):
                for b in range(4):
                    at_ = (half * 4 + b) * HEADS
                    src = l_d[half].rearrange("s (h t) -> h s t", h=HEADS)
                    pool.dma_start(blk[at_:at_ + HEADS], src[:, 32 * b:32 * b + 32, 32 * b:32 * b + 32]
                                   ).then_inc(s_blk, 16)
            for k in range(2):
                pool.wait_ge(s_ad[k], 64)
            pool.wait_ge(s_xd, 16)

            block_mask = consts[:, C_BD:C_BD + P].rearrange("p (b t) -> p b t", b=4)

            def dense(out, compact):
                o = out[:, 0:8 * P].rearrange("p (n b t) -> p n b t", n=8, b=4)
                c = compact[:].rearrange("p (n t) -> p n t", n=8).unsqueeze(2).to_broadcast([P, 8, 4, 32])
                pool.tensor_tensor(o, c, block_mask.unsqueeze(1).to_broadcast([P, 8, 4, 32]), ALU.mult
                                   ).then_inc(s_dense, 1)

            def load_inverses(j):
                if j:
                    pool.wait_ge(s_dense, 6 * j - 2)
                for k, tile in enumerate((xc, yc)):
                    src = inv_d[k][:, :, BATCH * j:BATCH * (j + 1), :].rearrange("s a h t -> s a (h t)")
                    pool.dma_start(tile[:].rearrange("p (a c) -> p a c", a=2), src).then_inc(s_cx[k], 16)

            def off_diagonal(col):
                mask = consts[:, col:col + P].unsqueeze(1).to_broadcast([P, BATCH, P])
                for half in range(2):
                    src = (l_x[:, 0:BATCH * T].rearrange("p (h t) -> p h t", h=BATCH)[:, :, 0:P] if half == 0 else
                           l_x[:, BATCH * T:PAIRS].rearrange("p (h t) -> p h t", h=BATCH))
                    out = t2[:, half * BATCH * P:(half + 1) * BATCH * P].rearrange("p (h t) -> p h t", h=BATCH)
                    pool.tensor_tensor(out, src, mask, ALU.mult).then_inc(s_dense, 1)

            for j in range(4):
                for k, (a, b) in enumerate(((0, BATCH * T), (BATCH * T, PAIRS))):
                    if j and k == 0:
                        pool.wait_ge(s_solve_pe, 8 * j - 2)
                    w = b - a
                    pool.dma_start(l_x[:, a:b], l_d[k][:, w * j:w * (j + 1)]).then_inc(s_lx[k], 16)
                if j == 0:
                    pool.wait_ge(s_invd, 16 * 16)
                    load_inverses(0)
                    pool.wait_ge(s_cx[0], 16)
                    dense(t1, xc)
                for k in range(2):
                    pool.wait_ge(s_lx[k], 16 * (j + 1))
                off_diagonal(C_M1)
                pool.wait_ge(s_cx[1], 16 * (j + 1))
                if j:
                    pool.wait_ge(s_solve_pe, 8 * j - 1)
                dense(t0, yc)
                if j:
                    pool.wait_ge(s_solve_pe, 8 * j)
                for k, (a, b) in enumerate(((0, BATCH * T), (BATCH * T, PAIRS))):
                    w = b - a
                    pool.dma_start(a_x[:, a:b], a_d[k][:, w * j:w * (j + 1)]).then_inc(s_ax[k], 16)
                pool.wait_ge(s_solve_pe, 8 * j + 1)
                off_diagonal(C_M2)
                if j < 3:
                    load_inverses(j + 1)
                    pool.wait_ge(s_cx[0], 16 * (j + 2))
                    pool.wait_ge(s_solve_pe, 8 * j + 3)
                    dense(t1, xc)
            pool.dma_start(bias_x.rearrange("p (h s) -> h p s", h=HEADS),
                           bass.AP(tensor=bias_d.tensor, offset=bias_d.offset + P, ap=[[REL, HEADS], [-1, P], [1, T]])
                           ).then_inc(s_bx, 16)
            pool.wait_ge(s_solve_pe, 32)
            pool.dma_start(xres[:], x_d).then_inc(s_xb, 16)
            for j in range(4):
                if j:
                    pool.wait_ge(s_biased, j)
                else:
                    pool.wait_ge(s_x1, 5)
                    pool.wait_ge(s_bx, 16)
                pool.dma_start(t4[:], bias_x[:, BATCH * T * j:BATCH * T * (j + 1)]).then_inc(s_bias, 16)

        @block.tensor
        def _(pe):
            def by_channel(out, kt, end, wh, wl, xh, xl):
                for m in range(GM):
                    to = out[:, m * T:(m + 1) * T]
                    ch = slice(m * P, (m + 1) * P)
                    nc.tensor.matmul(to, wh[:, ch], xh, start=kt == 0 and m % 2 == 0, stop=False,
                                     skip_group_check=True)
                    nc.tensor.matmul(to, wh[:, ch], xl, start=False, stop=False, skip_group_check=True)
                    last = nc.tensor.matmul(to, wl[:, ch], xh, start=False, stop=end and m % 2 == 1,
                                            skip_group_check=True)
                return last

            def by_token(out, kt, end, wh, wl, xh, xl):
                for half in range(2):
                    to, t = out[:, half * GC:(half + 1) * GC], slice(half * P, (half + 1) * P)
                    nc.tensor.matmul(to, xh[:, t], wh, start=kt == 0, stop=False)
                    nc.tensor.matmul(to, xh[:, t], wl, start=False, stop=False)
                    last = nc.tensor.matmul(to, xl[:, t], wh, start=False, stop=end)
                return last

            def group(free, n0, par, slot0, hi, lo, kt0=0, slabs=SLABS, ready=None,
                      fillers=None, products=by_channel):
                if free is not None:
                    pe.wait_ge(s_free, free.v)
                for s in range(slabs):
                    slot = (slot0 + s) % HL_SLOTS
                    pe.wait_ge(s_lo, (n0 + (s + 1)).v)
                    for kk in range(SLAB_K):
                        kt = s * SLAB_K + kk
                        if ready and (kt == 0 or ready(kt) != ready(kt - 1)):
                            pe.wait_ge(s_opnd, ready(kt))
                        row = slice(kk * GC, (kk + 1) * GC)
                        last = products(acc[:, par], kt, kt == slabs * SLAB_K - 1, w_hi[:, slot, row],
                                        w_lo[:, slot, row], hi[:, kt0 + kt], lo[:, kt0 + kt])
                    last.then_inc(s_used, 1)
                    if fillers and s in fillers:
                        fillers[s]()

            def partition_sums(src, out, first=True, last=True):
                for k in range(4):
                    ins = nc.tensor.matmul(out, ones, src[:, k * T:(k + 1) * T],
                                           start=first and k == 0, stop=last and k == 3)
                if last:
                    ins.then_inc(s_stat, 1)

            def mod_sums(pieces):
                for m in range(KT):
                    col = 512 * (m // (KT // pieces)) + m
                    last = nc.tensor.matmul(misc[:, col:col + 1], mod_acc[:, m * P:(m + 1) * P],
                                            ones[:, 0:1], start=True, stop=True)
                    if (m + 1) % (KT // pieces) == 0:
                        last.then_inc(s_mod_sum, 1)

            pe.wait_ge(s_con, 16)
            pe.wait_ge(s_sums, 1)
            partition_sums(t0, misc[:, 0:T])
            pe.wait_ge(s_mod_used, KT)
            pe.wait_ge(s_root, 1)
            mod_sums(1)
            pe.wait_ge(s_mod_used, 2 * KT)
            pe.wait_ge(s_shift, 1)
            mod_sums(4)

            group(None, Num(0), 0, 0, a_hi, a_lo, ready=lambda kt: kt + 1)
            group(None, Num(SLABS), 1, 0, a_hi, a_lo)
            with pe.Fori(1, 4) as i:
                for k in range(2):
                    group(Num(k - 1, i, 2), Num(k * SLABS, i, 2 * SLABS), k, 0, a_hi, a_lo)
            pe.wait_ge(s_gate, GATES)
            mod_sums(1)
            for j in range(4):
                group(Num(G_GRP + j - 1), Num(N_GRP + j * GRP_SLABS), j % 2, j * GRP_SLABS, b_hi, b_lo,
                      kt0=4 * j, slabs=GRP_SLABS, ready=lambda kt: O_H + j + 1)
            def early_sums():
                pe.wait_ge(s_sums, 4)
                partition_sums(t3, misc[:, 0:T], last=False)
                pe.wait_ge(s_sums, 5)
                partition_sums(t4, misc[:, 512:512 + T], last=False)

            for j in range(4):
                g = Num(G_WOUT + j)
                group(g + (-1), slab_of(g), j % 2, N_WOUT % HL_SLOTS, a_hi, a_lo,
                      ready=lambda kt: O_POOLED + kt // 4 + 1, fillers={6: early_sums} if j == 3 else None)
            pe.wait_ge(s_sq, 4 + 16)
            partition_sums(t0, misc[:, 0:T], first=False)
            pe.wait_ge(s_sq, 4 + 20)
            partition_sums(t1, misc[:, 512:512 + T], first=False)

            def operand_b(kt):
                return O_Z + kt + 1

            def pairs(lhs, rhs, done, also=None):
                for h in range(BATCH):
                    k = h * T
                    nc.tensor.matmul(misc[:, k:k + T], lhs(h, 0), rhs(h, 0, T), start=True, stop=also is None)
                    if also:
                        nc.tensor.matmul(misc[:, k + P:k + T], also, rhs(h, 1, P), start=False, stop=True)
                    k = BATCH * T + h * P
                    last = nc.tensor.matmul(misc[:, k:k + P], lhs(h, 1), rhs(h, 1, P), start=True, stop=True)
                last.then_inc(done, 1)

            def head_sums(n, src, at_=0):
                pe.wait_ge(s_sq2, n.v)
                for h in range(BATCH):
                    last = nc.tensor.matmul(misc[:, at_ + h * T:at_ + (h + 1) * T], ones, src[:, h * T:(h + 1) * T],
                                            start=True, stop=True)
                last.then_inc(s_nrm, 1)

            def split_sums(n):
                pe.wait_ge(s_ones, 1)
                pe.wait_ge(s_sql, n.v)
                for h in range(BATCH):
                    out, of = misc[:, h * T:(h + 1) * T], slice(h * T, (h + 1) * T)
                    nc.tensor.matmul(out, ones_r[:], sq_hi[:, of], start=True, stop=False)
                    last = nc.tensor.matmul(out, ones_r[:], sq_lo[:, of], start=False, stop=True)
                last.then_inc(s_nrm, 1)

            def log_decays(i):
                pe.wait_ge(s_rinv, Num(1, i, 2).v)
                pe.wait_ge(s_gu, Num(8, i, 8).v)
                later = consts[:, C_GT:C_GT + P]

                def rhs(h, half, w):
                    k = h * T if half == 0 else BATCH * T + h * P
                    return gu_t[:, k:k + w]

                pairs(lambda h, half: later, rhs, s_dm, also=ones)

            def key_products(i, q, done):
                def rhs(h, half, w):
                    return q[:, h * T + half * P:h * T + half * P + w]

                pairs(lambda h, half: k_n[:, h * T + half * P:h * T + half * P + P], rhs, done)

            def key_key(i):
                pe.wait_ge(s_qkn, Num(2, i, 2).v)
                key_products(i, k_n, s_kk)

            def key_query(i):
                pe.wait_ge(s_l, Num(1, i, 1).v)
                key_products(i, q_n, s_qk)

            def decay_and_beta():
                pe.wait_ge(s_ab_lo, 1)
                pe.wait_ge(s_opnd, operand_b(KT - 1))
                for kt in range(KT):
                    wh, wl = (w[:, kt * 2 * HEADS:(kt + 1) * 2 * HEADS] for w in (ab_hi, ab_lo))
                    out = misc[0:2 * HEADS, 1536:1536 + T]
                    nc.tensor.matmul(out, wh, b_hi[:, kt], start=kt == 0, stop=False)
                    nc.tensor.matmul(out, wh, b_lo[:, kt], start=False, stop=False)
                    last = nc.tensor.matmul(out, wl, b_hi[:, kt], start=False, stop=kt == KT - 1)
                last.then_inc(s_ab_mm, 1)

            g = Num(G_A)
            group(g + (-1), slab_of(g), 0, 0, b_hi, b_lo, ready=operand_b, fillers={6: decay_and_beta})
            pe.wait_ge(s_ab_dve, 1)
            for half in range(2):
                at_ = 1536 + half * 2 * HEADS
                last = nc.tensor.transpose(misc[:, at_:at_ + 2 * HEADS], ab_c[0:2 * HEADS, half * P:(half + 1) * P],
                                           ident[0:2 * HEADS, 0:2 * HEADS])
            last.then_inc(s_ab_mm, 1)
            with pe.Fori(0, 4) as i:
                g = Num(G_A + 1, i, 2)
                group(g + (-1), slab_of(g), 1, 0, b_hi, b_lo, fillers={
                    3: lambda: head_sums(Num(1, i, 2), t2), 6: lambda: log_decays(i)})
                g = g + 1
                group(g + (-1), slab_of(g), 0, 0, b_hi, b_lo, fillers={
                    3: lambda: head_sums(Num(2, i, 2), t2), 5: lambda: key_key(i), 6: lambda: key_query(i)})
            for k in range(9, 12):
                g = Num(G_A + k)
                group(g + (-1), slab_of(g), k % 2, 0, b_hi, b_lo)

            def tile_of(t, half, h):
                k = (half * BATCH + h) * P
                return t[:, k:k + P]

            def eight(bank, lhs, rhs):
                for half in range(2):
                    for h in range(BATCH):
                        k = 1024 * bank + (half * BATCH + h) * P
                        last = nc.tensor.matmul(misc[:, k:k + P], tile_of(lhs, half, h), tile_of(rhs, half, h),
                                                start=True, stop=True)
                return last

            def value(j, h, half):
                return vo[:, BATCH * j + h, half * P:(half + 1) * P]

            def solve(j, step):
                done = None
                if step == 0:
                    pe.wait_ge(s_dense, 6 * j + 3)
                    if j:
                        pe.wait_ge(s_solve_act, 6 * j)
                    done = eight(0, t2, t1)
                elif step == 1:
                    pe.wait_ge(s_solve_act, 6 * j + 1)
                    pe.wait_ge(s_dense, 6 * j + 4)
                    eight(1, t3, t0)
                    done = eight(0, t0, t3)
                elif step == 2:
                    pe.wait_ge(s_solve_dve, 3 * j + 1)
                    pe.wait_ge(s_dense, 6 * j + 6)
                    eight(0, t2, t1)
                    for h in range(BATCH):
                        for half in range(2):
                            k = 1024 + h * T + half * P
                            done = nc.tensor.transpose(misc[:, k:k + P], value(j, h, half), ident)
                elif step == 3:
                    pe.wait_ge(s_solve_act, 6 * j + 3)
                    done = eight(1, t3, t0)
                elif step == 4:
                    pe.wait_ge(s_solve_dve, 3 * j + 2)
                    for h in range(BATCH):
                        done = nc.tensor.matmul(misc[:, h * P:(h + 1) * P], tile_of(t0, 0, h), value(j, h, 0),
                                                start=True, stop=True)
                elif step == 5:
                    pe.wait_ge(s_solve_act, 6 * j + 4)
                    for h in range(BATCH):
                        done = nc.tensor.matmul(misc[:, 512 + h * P:512 + (h + 1) * P],
                                                l_x[:, h * T + P:(h + 1) * T], value(j, h, 0),
                                                start=True, stop=True)
                elif step == 6:
                    pe.wait_ge(s_solve_dve, 3 * j + 3)
                    for h in range(BATCH):
                        done = nc.tensor.matmul(misc[:, h * P:(h + 1) * P], tile_of(t0, 1, h), value(j, h, 1),
                                                start=True, stop=True)
                else:
                    pe.wait_ge(s_solve_act, 6 * j + 5)
                    for k in range(2):
                        pe.wait_ge(s_ax[k], 16 * (j + 1))
                    for h in range(BATCH):
                        nc.tensor.matmul(misc[:, h * T:(h + 1) * T], value(j, h, 0), a_x[:, h * T:(h + 1) * T],
                                         start=True, stop=False)
                        k = BATCH * T + h * P
                        done = nc.tensor.matmul(misc[:, h * T + P:(h + 1) * T], value(j, h, 1), a_x[:, k:k + P],
                                                start=False, stop=True)
                done.then_inc(s_solve_pe, 1)

            for j in range(4):
                g = Num(G_A + 12 + j)
                fill = {s: (lambda s=s: solve(j, s)) for s in range(8)}
                if j:
                    fill[4] = lambda: (solve(j, 4), head_sums(Num(8 + j), t4, 1024))
                group(g + (-1), slab_of(g), j % 2, 0, b_hi, b_lo, fillers=fill)
            def early_sums_b():
                pe.wait_ge(s_sums, 7)
                partition_sums(t3, misc[:, 0:T], last=False)

            for j in range(4):
                g = Num(G_AOUT + j)
                group(g + (-1), slab_of(g), j % 2, 0, a_hi, a_lo, ready=lambda kt: O_A + kt // 4 + 1,
                      fillers={0: {0: lambda: head_sums(Num(12), t4, 1024)}, 3: {6: early_sums_b}}.get(j))
            pe.wait_ge(s_sq, 24 + 4)
            partition_sums(t0, misc[:, 0:T], first=False)

            def scores(i):
                pe.wait_ge(s_bn, Num(2, i, 2).v)
                for h in range(BATCH):
                    k = h * T
                    nc.tensor.matmul(misc[:, k:k + T], t2[:, k + P:k + T], t0[:, k:k + T], start=True, stop=True)
                    at_ = BATCH * T + h * P
                    last = nc.tensor.matmul(misc[:, at_:at_ + P], t2[:, k:k + P], t0[:, k:k + P],
                                            start=True, stop=True)
                last.then_inc(s_score, 1)

            def transposed(i):
                pe.wait_ge(s_pn, Num(1, i, 1).v)
                for h in range(BATCH):
                    k, at_ = h * T, BATCH * T + h * P
                    nc.tensor.transpose(misc[:, k:k + P], p_t[:, at_:at_ + P], ident)
                    nc.tensor.transpose(misc[:, k + P:k + T], p_t[:, k:k + P], ident)
                    last = nc.tensor.transpose(misc[:, at_:at_ + P], p_t[:, k + P:k + T], ident)
                last.then_inc(s_pt, 1)

            def attended(i):
                pe.wait_ge(s_vn, Num(1, i, 1).v)
                pe.wait_ge(s_ptc_act, Num(1, i, 1).v)
                pe.wait_ge(s_ptc_dve, Num(1, i, 1).v)
                for h in range(BATCH):
                    k, at_ = h * T, BATCH * T + h * P
                    nc.tensor.matmul(misc[:, k:k + T], v_n[:, 0, h * P:(h + 1) * P], p_tt[:, k:k + T],
                                     start=True, stop=False)
                    last = nc.tensor.matmul(misc[:, k + P:k + T], v_n[:, 1, h * P:(h + 1) * P],
                                            p_tt[:, at_:at_ + P], start=False, stop=True)
                last.then_inc(s_pv, 1)

            with pe.Fori(0, 4) as i:
                g = Num(G_B, i, 4)
                group(g + (-1), slab_of(g), 0, 0, b_hi, b_lo, ready=lambda kt: O_AO + kt + 1)
                g = g + 1
                group(g + (-1), slab_of(g), 1, 0, b_hi, b_lo, fillers={
                    3: lambda: split_sums(Num(1, i, 2))})
                g = g + 1
                group(g + (-1), slab_of(g), 0, 0, b_hi, b_lo, products=by_token, fillers={
                    3: lambda: split_sums(Num(2, i, 2)), 6: lambda: scores(i)})
                g = g + 1
                group(g + (-1), slab_of(g), 1, 0, b_hi, b_lo, fillers={
                    4: lambda: transposed(i), 6: lambda: attended(i)})
            for j in range(4):
                g = Num(G_BOUT + j)
                group(g + (-1), slab_of(g), j % 2, 0, a_hi, a_lo, ready=lambda kt: O_B + kt // 4 + 1)

        def stream_of(n):
            return n + GATES if n.var is not None or n.c >= N_GRP else Num(n.c // 2 * 3 + n.c % 2)

        def wide(t, k0=0):
            return t[:, k0:k0 + 4].rearrange("p k t -> p (k t)")

        def halves_of_pairs():
            return (1, 0, T), (0, BATCH * T, P)

        @block.scalar
        def _(act):
            own = Own(s_hi)

            def hi_parts(n, count):
                for k in range(count):
                    m = n + k
                    if m.var is None and m.c >= N_SLABS:
                        return
                    q = stream_of(m)
                    act.wait_ge(s_raw[q.c % RAW_SLOTS],
                                Num(16 * (q.c // RAW_SLOTS + 1), q.var, 16 * q.mul // RAW_SLOTS).v)
                    if m.var is not None or m.c >= HL_SLOTS:
                        act.wait_ge(s_used, (m + (1 - HL_SLOTS)).v)
                    nc.scalar.activation(w_hi[:, m.c % HL_SLOTS], raw[:, q.c % RAW_SLOTS],
                                                 ACT.Copy).then_inc(own.up(s_hi), 1)

            def round_tiles(out, src, ready, bias=None):
                act.wait_ge(s_tmp, ready)
                if bias is None:
                    ins = nc.scalar.activation(out, src, ACT.Copy)
                else:
                    ins = nc.scalar.activation(out, src, ACT.Identity, bias=bias)
                ins.then_inc(own.up(s_rnd), 1)

            def rsqrt(out, src, done, scale=1.0, power=0.0):
                nc.scalar.activation(out, src, ACT.Ln, bias=eps, scale=scale).then_inc(own.up(s_act), 1)
                act.wait_ge(*own.last())
                nc.scalar.activation(out, out, ACT.Exp, bias=power, scale=-0.5).then_inc(own.up(done), 1)

            act.wait_ge(s_vec, 16)
            nc.scalar.activation(silu_c[:], vecs[:, V_C:V_C + KT], ACT.Silu).then_inc(own.up(s_silu_c), 1)
            act.wait_ge(s_x, 16)
            act.wait_ge(s_eps, 2)
            for j, t in enumerate((t0, t1, t2, t1)):
                if j == 3:
                    act.wait_ge(s_dve, 1)
                nc.scalar.activation(t[:, 0:4 * T], wide(xres, 4 * j), ACT.Square).then_inc(own.up(s_sq), 1)
            act.wait_ge(s_stat, 1)
            rsqrt(r1[:], misc[:, 0:T], s_root, scale=1.0 / D)
            hi_parts(Num(0), 2)
            for j in range(4):
                for m in range(GM):
                    kt = GM * j + m
                    round_tiles(a_hi[:, kt], tiles(t2)[:, m], kt + 1, bias=modv[:, kt:kt + 1])
                hi_parts(Num(2 + 2 * j), 2)
            hi_parts(Num(10), AHEAD - 10)

            for j in range(4):
                act.wait_ge(s_used, (2 * j + 1) * SLABS)
                if j == 0:
                    act.wait_ge(s_pads, 1)
                else:
                    act.wait_ge(s_opnd, O_H + j)
                nc.scalar.activation(tiles(t0, 4, UW)[:, :, PAD:PAD + T], tiles(acc[:, 0]), ACT.Copy
                    ).then_inc(own.up(s_act_read), 1)
                hi_parts(Num(AHEAD + 16 * j), 5)
                round_tiles(wide(b_hi, 4 * j), (t2, t1)[j % 2][:, 0:4 * T], KT + 1 + j)
                hi_parts(Num(AHEAD + 16 * j + 5), 3)
                act.wait_ge(s_used, (2 * j + 2) * SLABS)
                nc.scalar.activation(wide(vo, 4 * j), acc[:, 1], ACT.Silu).then_inc(own.up(s_act_read), 1)
                if j < 3:
                    hi_parts(Num(AHEAD + 16 * j + 8), 8)
            hi_parts(Num(N_GRP + 7), 2)
            for j in range(4):
                round_tiles(wide(a_hi, 4 * j), (t1, t2)[j % 2][:, 0:4 * T], O_POOLED + 1 + j)
                hi_parts(Num(N_GRP + 9 + 2 * j), 2)
            hi_parts(Num(N_WOUT + 9), 6)

            for j in range(4):
                if j == 2:
                    act.wait_ge(s_ab, 16)
                    nc.scalar.activation(ab_hi[:], ab_raw[:], ACT.Copy).then_inc(own.up(s_ab_hi), 1)
                act.wait_ge(s_x1, j + 1)
                if j >= 2:
                    act.wait_ge(s_sums, 2 * j - 1)
                plain, weighed = (t3, t4) if j == 0 else (t0, t1)
                nc.scalar.activation(plain[:, 0:4 * T], wide(xres, 4 * j), ACT.Square).then_inc(own.up(s_sq), 1)
                for m in range(GM):
                    nc.scalar.activation(tiles(weighed)[:, m], xres[:, 4 * j + m], ACT.Square,
                                                 scale=vecs[:, V_FG + 4 * j + m:V_FG + 4 * j + m + 1]
                                                     ).then_inc(own.up(s_sq), 1)
                if j == 3:
                    act.wait_ge(s_stat, 2)
                    rsqrt(r1[:], misc[:, 0:T], s_root, scale=1.0 / D)
                    act.wait_ge(s_var2, 1)
                    rsqrt(r2[:], r2[:], s_root, scale=1.0 / D)
                    for kt in range(KT):
                        round_tiles(b_hi[:, kt], tiles(t2)[:, kt % 4], O_Z + kt + 1)
                hi_parts(slab_of(Num(G_WOUT + j)) + AHEAD, SLABS)

            act.wait_ge(s_ab_dve, 4)
            nc.scalar.activation(ab_t[:, 2], ab_t[:, 1], ACT.Exp).then_inc(own.up(s_ab_act), 1)
            nc.scalar.activation(ab_t[:, 3].rearrange("p (a h) -> p a h", a=2),
                                         misc[:, 1536:1600].rearrange("p (a h) -> p a h", a=2)[:, :, HEADS:],
                                         ACT.Exp, scale=-1.0).then_inc(own.up(s_ab_act), 1)
            nc.scalar.activation(ab_t[:, 4, 0:HEADS], vecs[:, V_ALOG:V_ALOG + HEADS], ACT.Exp
                ).then_inc(own.up(s_ab_act), 1)
            act.wait_ge(*own.last(3))
            nc.scalar.activation(ab_t[:, 2], ab_t[:, 2], ACT.Ln, bias=1.0).then_inc(own.up(s_ab_act), 1)

            def first_tap(g, par, to):
                act.wait_ge(s_used, slab_of(g + 1).v)
                act.wait_ge(*own.last())
                for m in range(GM):
                    col = (g + (-G_A)).times(16) + (V_CONV + 4 * m + 3)
                    nc.scalar.activation(tiles(to)[:, m], acc[:, par, m * T:(m + 1) * T], ACT.Copy,
                                                 scale=vecs[:, bass.ds(col.v, 1)]).then_inc(own.up(s_tap), 1)

            def norm_inputs(g):
                act.wait_ge(s_free, (g + 1).v)
                nc.scalar.activation(t1[:, 0:4 * T], t0[:, 0:4 * T], ACT.Silu).then_inc(own.up(s_act), 1)
                act.wait_ge(*own.last())
                nc.scalar.activation(t2[:, 0:4 * T], t1[:, 0:4 * T], ACT.Square).then_inc(own.up(s_sq2), 1)

            with act.Fori(0, 4) as i:
                own.enter(i, {s_tap: 8, s_act: 4, s_sq2: 2, s_rinv: 2, s_e: 1, s_hi: 16})
                for k, power in ((0, log_q), (1, 0.0)):
                    g = Num(G_A + k, i, 2)
                    n = slab_of(g) + AHEAD
                    first_tap(g, k, t0)
                    hi_parts(n, 2)
                    norm_inputs(g)
                    hi_parts(n + 2, 2)
                    act.wait_ge(s_nrm, Num(1 + k, i, 2).v)
                    rsqrt(t3[:], misc[:, 0:1024], s_rinv, power=power)
                    hi_parts(n + 4, 3)
                    if k == 0:
                        act.wait_ge(s_dm, Num(1, i, 1).v)
                        nc.scalar.activation(dec_t[:], misc[:, 0:PAIRS], ACT.Exp).then_inc(own.up(s_e), 1)
                    hi_parts(n + 7, 1)
                own.leave(4)

            def solve_copies(j, step):
                out = {0: (t3[:], misc[:, 0:1024]),
                       4: (vo[:, BATCH * j:BATCH * (j + 1), 0:P],
                           misc[:, 0:512].rearrange("p (h t) -> p h t", h=BATCH)),
                       6: (vo[:, BATCH * j:BATCH * (j + 1), P:T],
                           misc[:, 0:512].rearrange("p (h t) -> p h t", h=BATCH)),
                       7: (wide(vo, BATCH * j), misc[:, 0:1024])}
                if step == 2:
                    act.wait_ge(s_solve_pe, 8 * j + 3)
                    nc.scalar.activation(t3[:], misc[:, 0:1024], ACT.Copy).then_inc(own.up(s_solve_act), 1)
                    nc.scalar.activation(wide(vo, BATCH * j), misc[:, 1024:2048], ACT.Copy
                        ).then_inc(own.up(s_solve_act), 1)
                elif step in out:
                    act.wait_ge(s_solve_pe, 8 * j + step + 1)
                    nc.scalar.activation(*out[step], ACT.Copy).then_inc(own.up(s_solve_act), 1)

            for g in range(G_A + 8, G_AOUT):
                n = slab_of(Num(g)) + AHEAD
                j = g - G_A - 12
                act.wait_ge(*own.last())
                if j < 0:
                    first_tap(Num(g), g % 2, t4)
                else:
                    nc.scalar.activation(t4[:], wide(vo, BATCH * j), ACT.Square).then_inc(own.up(s_sq2), 1)
                for k in range(8):
                    if j < 0 and k == 1:
                        act.wait_ge(s_free, g + 1)
                        nc.scalar.activation(wide(vo, 4 * (g - G_A - 8)), t4[:], ACT.Silu
                            ).then_inc(own.up(s_vt), 1)
                    if g >= G_A + 11 and g < G_AOUT - 1 and k:
                        solve_copies(j + 1, k - 1)
                    last = g == G_AOUT - 1
                    if j >= 0 and k == (1 if last else 5):
                        act.wait_ge(s_nrm, 9 + j)
                        rsqrt(t4[:], misc[:, 1024:2048], s_rinv, scale=1.0 / P)
                    if j >= 0 and k == (2 if last else 6):
                        act.wait_ge(s_on, j + 1)
                        act.wait_ge(s_used, slab_of(Num(g + 1)).c)
                        nc.scalar.activation(t4[:], acc[:, g % 2], ACT.Silu).then_inc(own.up(s_zs), 1)
                    if j >= 0 and k == (3 if last else 7):
                        round_tiles(wide(a_hi, 4 * j), wide(vo, 4 * j), O_A + 1 + j)
                    hi_parts(n + k, 1)
                if g >= G_A + 11 and g < G_AOUT - 1:
                    solve_copies(j + 1, 7)

            nc.scalar.activation(ones_r[:], ones, ACT.Copy).then_inc(own.up(s_ones), 1)
            for j in range(4):
                act.wait_ge(s_x1, 4 + j + 1)
                if j >= 2:
                    act.wait_ge(s_sums, 4 + j)
                act.wait_ge(*own.last())
                nc.scalar.activation((t3 if j == 0 else t0)[:, 0:4 * T], wide(xres, 4 * j), ACT.Square
                    ).then_inc(own.up(s_sq), 1)
                if j == 3:
                    act.wait_ge(s_stat, 4)
                    rsqrt(r1[:], misc[:, 0:T], s_root, scale=1.0 / D)
                    for kt in range(KT):
                        round_tiles(b_hi[:, kt], tiles(t2)[:, kt % 4], O_AO + kt + 1)
                hi_parts(slab_of(Num(G_AOUT + j)) + AHEAD, SLABS)

            with act.Fori(0, 4) as i:
                own.enter(i, {s_act: 11, s_sq2: 2, s_sqh: 2, s_rinv: 2, s_vn: 1, s_prob: 1, s_ptc_act: 1, s_zb: 1,
                              s_rnd: 1, s_hi: 32})
                for k, power in ((0, log_q), (1, 0.0)):
                    g = Num(G_B + k, i, 4)
                    n = slab_of(g) + AHEAD
                    if k:
                        act.wait_ge(s_bn, Num(1, i, 2).v)
                    else:
                        act.wait_ge(s_opnd, Num(O_B, i, 1).v)
                    act.wait_ge(s_used, slab_of(g + 1).v)
                    nc.scalar.activation(t0[:, 0:4 * T], acc[:, k], ACT.Copy).then_inc(own.up(s_act), 1)
                    nc.scalar.activation(t1[:, 0:4 * T], acc[:, k], ACT.Square).then_inc(own.up(s_sq2), 1)
                    act.wait_ge(*own.last())
                    nc.scalar.activation(sq_hi[:], t1[:, 0:4 * T], ACT.Copy).then_inc(own.up(s_sqh), 1)
                    hi_parts(n, 4)
                    act.wait_ge(s_nrm, Num(13 + k, i, 2).v)
                    rsqrt(t3[:], misc[:, 0:1024], s_rinv, scale=1.0 / P, power=power)
                    hi_parts(n + 4, 4)
                g = Num(G_B + 2, i, 4)
                n = slab_of(g) + AHEAD
                act.wait_ge(s_used, slab_of(g + 1).v)
                nc.scalar.activation(v_n[:].rearrange("p a c -> p (a c)"), acc[:, 0], ACT.Copy
                    ).then_inc(own.up(s_vn), 1)
                hi_parts(n, 2)
                act.wait_ge(s_max, Num(1, i, 1).v)
                for half, k, w in halves_of_pairs():
                    for h in range(BATCH):
                        at_ = k + h * w
                        last = (half, h) == (0, BATCH - 1)
                        nc.scalar.activation(p_t[:, at_:at_ + w], p_t[:, at_:at_ + w], ACT.Exp,
                                                     bias=row_max[:, half, h:h + 1],
                                                     accum_out=row_sum[:, half, h:h + 1]
                                                         ).then_inc(own.up(s_prob if last else s_act), 1)
                hi_parts(n + 2, 4)
                act.wait_ge(s_pt, Num(1, i, 1).v)
                nc.scalar.activation(p_tt[:, 0:BATCH * T], misc[:, 0:BATCH * T], ACT.Copy
                    ).then_inc(own.up(s_ptc_act), 1)
                hi_parts(n + 6, 2)
                g = g + 1
                act.wait_ge(s_used, slab_of(g + 1).v)
                nc.scalar.activation(t1[:, 0:4 * T], acc[:, 1], ACT.Silu).then_inc(own.up(s_zb), 1)
                hi_parts(slab_of(g) + AHEAD, 2)
                act.wait_ge(s_tmp, Num(O_B + 1, i, 1).v)
                nc.scalar.activation(a_hi[:, bass.ds(i * 4, 4)].rearrange("p k t -> p (k t)"),
                                             t1[:, 0:4 * T], ACT.Copy).then_inc(own.up(s_rnd), 1)
                hi_parts(slab_of(g) + (AHEAD + 2), 6)
                own.leave(4)
            for j in range(4):
                hi_parts(slab_of(Num(G_BOUT + j)) + AHEAD, SLABS)

        @block.vector
        def _(dve):
            own = Own(s_lo)

            def add_gate(k):
                q = 3 * k + 2
                dve.wait_ge(s_raw[q % RAW_SLOTS], 16 * (q // RAW_SLOTS + 1))
                half = mod_acc[:, k % 2 * (D // 2):(k % 2 + 1) * (D // 2)]
                if k >= 2:
                    dve.wait_ge(s_gate, k - 1)
                    ins = nc.vector.scalar_tensor_tensor(out=half, in0=raw[:, q % RAW_SLOTS],
                                                         scalar=silu_c[:, k // 2:k // 2 + 1], in1=half,
                                                         op0=ALU.mult, op1=ALU.add)
                else:
                    dve.wait_ge(s_mod_sum, 5)
                    ins = nc.vector.tensor_scalar(half, raw[:, q % RAW_SLOTS], silu_c[:, 0:1], None, ALU.mult)
                ins.then_inc(own.up(s_gate), 1)

            def lo_parts(n, count):
                for k in range(count):
                    m = n + k
                    if m.var is None and m.c >= N_SLABS:
                        return
                    if m.var is None and m.c < N_GRP and m.c % 2 == 0 and m.c:
                        add_gate(m.c // 2 - 1)
                    if m.var is None and m.c == N_GRP:
                        add_gate(GATES - 1)
                    q = stream_of(m)
                    slot = m.c % HL_SLOTS
                    dve.wait_ge(s_hi, (m + 1).v)
                    nc.vector.tensor_tensor(w_lo[:, slot], raw[:, q.c % RAW_SLOTS],
                                                    w_hi[:, slot].bitcast(F32), ALU.subtract
                                                        ).then_inc(own.up(s_lo), 1)

            def lo_tiles(out_lo, src, hi, rounded, bias=None):
                dve.wait_ge(s_rnd, rounded)
                if bias is None:
                    ins = nc.vector.tensor_tensor(out_lo, src, hi.bitcast(F32), ALU.subtract)
                else:
                    ins = nc.vector.scalar_tensor_tensor(out=out_lo, in0=src, scalar=bias, in1=hi.bitcast(F32),
                                                         op0=ALU.add, op1=ALU.subtract)
                ins.then_inc(own.up(s_opnd), 1)

            def add(out, in0, in1, op=ALU.add, done=None):
                nc.vector.tensor_tensor(out, in0, in1, op).then_inc(own.up(done or s_dve), 1)

            def scaled(out, src, scalar, row, done=None):
                nc.vector.scalar_tensor_tensor(out=out, in0=src, scalar=scalar, in1=row,
                                                       op0=ALU.mult, op1=ALU.mult
                                                           ).then_inc(own.up(done or s_dve), 1)

            dve.wait_ge(s_silu_c, 1)
            for i in range(2 * KT):
                dve.wait_ge(s_mod[i % MOD_SLOTS], 16 * (i // MOD_SLOTS + 1))
                if i % KT == 0:
                    if i:
                        dve.wait_ge(s_mod_sum, 1)
                        add(modv[:, 0:KT], misc[:, 0:KT], vecs[:, V_BMOD:V_BMOD + KT], done=s_shift)
                    ins = nc.vector.tensor_scalar(mod_acc[:], mod_ring[:, i % MOD_SLOTS], silu_c[:, 0:1], None,
                                                  ALU.mult)
                else:
                    dve.wait_ge(s_mod_used, i)
                    ins = nc.vector.scalar_tensor_tensor(out=mod_acc[:], in0=mod_ring[:, i % MOD_SLOTS],
                                                         scalar=silu_c[:, i % KT:i % KT + 1], in1=mod_acc[:],
                                                         op0=ALU.mult, op1=ALU.add)
                ins.then_inc(own.up(s_mod_used), 1)
                if i == 3:
                    for k, t in enumerate((t1, t2, t1)):
                        dve.wait_ge(s_sq, k + 2)
                        if k:
                            dve.wait_ge(*own.last())
                        add(t0[:, 0:4 * T], t0[:, 0:4 * T], t[:, 0:4 * T], done=s_sums if k == 2 else None)
            lo_parts(Num(0), 2)
            for j in range(4):
                cols = slice(KT + GM * j, KT + GM * (j + 1))
                col = 512 * j + GM * j
                dve.wait_ge(s_mod_sum, 2 + j)
                dve.wait_ge(*own.last())
                nc.vector.scalar_tensor_tensor(
                    out=modv[:, cols], in0=misc[:, col:col + GM], scalar=1.0,
                    in1=vecs[:, V_BMOD + cols.start:V_BMOD + cols.stop], op0=ALU.add, op1=ALU.add
                        ).then_inc(own.up(s_dve), 1)
                dve.wait_ge(*own.last())
                dve.wait_ge(s_root, 1)
                for m in range(GM):
                    kt = GM * j + m
                    scaled(tiles(t2)[:, m], xres[:, kt], modv[:, KT + kt:KT + kt + 1], r1[:], s_tmp)
                for m in range(GM):
                    kt = GM * j + m
                    lo_tiles(a_lo[:, kt], tiles(t2)[:, m], a_hi[:, kt], kt + 1, bias=modv[:, kt:kt + 1])
                lo_parts(Num(2 + 2 * j), 2)
            lo_parts(Num(10), AHEAD - 10)

            for j, w in enumerate(WINDOWS):
                dve.wait_ge(s_act_read, 2 * j + 1)
                dve.wait_ge(*own.last())
                u = tiles(t0, 4, UW)
                src, dst, other = u, tiles(t1, 4, UW), tiles(t2, 4, UW)
                reach, d = UW, 1
                while d < w:
                    reach -= d
                    add(dst[:, :, 0:reach], src[:, :, 0:reach], src[:, :, d:d + reach],
                        done=s_free if d == 1 else s_dve)
                    dve.wait_ge(*own.last())
                    src, dst, other = dst, other, dst
                    d *= 2
                sums = src[:, :, PAD - w // 2:PAD - w // 2 + T]
                own_u = u[:, :, PAD:PAD + T]
                pooled = tiles((t2, t1)[j % 2])
                nc.vector.scalar_tensor_tensor(out=pooled, in0=sums, scalar=1.0 / w, in1=own_u,
                                                       op0=ALU.mult, op1=ALU.subtract
                                                           ).then_inc(own.up(s_dve), 1)
                dve.wait_ge(*own.last())
                for k, (lo, ins_at) in enumerate(((0, 0), (T - PAD, PAD))):
                    edge = pooled[:, :, lo:lo + PAD]
                    share = vecs[:, V_EDGE + 2 * PAD * j + ins_at:V_EDGE + 2 * PAD * j + ins_at + PAD]
                    add(edge, sums[:, :, lo:lo + PAD], share.unsqueeze(1).to_broadcast([P, 4, PAD]), ALU.mult)
                    dve.wait_ge(*own.last())
                    add(edge, edge, own_u[:, :, lo:lo + PAD], ALU.subtract, done=s_tmp if k else None)
                lo_parts(Num(AHEAD + 16 * j), 5)
                lo_tiles(wide(b_lo, 4 * j), (t2, t1)[j % 2][:, 0:4 * T], wide(b_hi, 4 * j), KT + 1 + j)
                lo_parts(Num(AHEAD + 16 * j + 5), 3)
                dve.wait_ge(s_act_read, 2 * j + 2)
                dve.sem_inc(own.also(s_free), 1)
                if j < 3:
                    lo_parts(Num(AHEAD + 16 * j + 8), 8)
            lo_parts(Num(N_GRP + 7), 2)
            dve.wait_ge(s_mod_sum, 6)
            add(modv[:, 2 * KT:3 * KT], misc[:, 0:KT],
                vecs[:, V_BMOD + 2 * KT:V_BMOD + 3 * KT])
            for j in range(4):
                z = (t1, t2)[j % 2]
                dve.wait_ge(s_used, N_GRP + GRP_SLABS * (j + 1))
                for m in range(GM):
                    scaled(tiles(z)[:, m], acc[:, j % 2, m * T:(m + 1) * T],
                           vecs[:, V_PSC + 4 * j + m:V_PSC + 4 * j + m + 1], vo[:, 4 * j + m],
                           done=s_tmp if m == 3 else None)
                lo_tiles(wide(a_lo, 4 * j), z[:, 0:4 * T], wide(a_hi, 4 * j), O_POOLED + 1 + j)
                dve.sem_inc(own.also(s_free), 1)
                lo_parts(Num(N_GRP + 9 + 2 * j), 2)
            lo_parts(Num(N_WOUT + 9), 6)

            for j in range(4):
                dve.wait_ge(s_used, slab_of(Num(G_WOUT + j + 1)).c)
                dve.wait_ge(*own.last())
                for m in range(GM):
                    kt = 4 * j + m
                    nc.vector.scalar_tensor_tensor(
                        out=xres[:, kt], in0=acc[:, j % 2, m * T:(m + 1) * T],
                        scalar=modv[:, 2 * KT + kt:2 * KT + kt + 1], in1=xres[:, kt],
                        op0=ALU.mult, op1=ALU.add).then_inc(own.up(s_x1 if m == 3 else s_dve), 1)
                dve.sem_inc(own.also(s_free), 1)
                if j in (1, 2):
                    dve.wait_ge(s_sq, 4 + 5 * j + 1)
                    add(t3[:], t3[:], t0[:, 0:4 * T], done=s_sums)
                    dve.wait_ge(s_sq, 4 + 5 * j + 5)
                    add(t4[:], t4[:], t1[:, 0:4 * T], done=s_sums)
                if j == 3:
                    dve.wait_ge(s_root, 2)
                    dve.wait_ge(s_stat, 3)
                    add(r2[:], misc[:, 512:512 + T], r1[:], ALU.mult)
                    dve.wait_ge(*own.last())
                    add(r2[:], r2[:], r1[:], ALU.mult, done=s_var2)
                    add(gains[:], vecs[:, V_FG:V_FG + KT], vecs[:, V_NW0:V_NW0 + KT], ALU.mult)
                    dve.wait_ge(s_root, 3)
                    add(r2[:], r2[:], r1[:], ALU.mult)
                    for q in range(4):
                        dve.wait_ge(*own.last())
                        for m in range(GM):
                            kt = 4 * q + m
                            scaled(tiles(t2)[:, m], xres[:, kt], gains[:, kt:kt + 1], r2[:], s_tmp)
                        for m in range(GM):
                            kt = 4 * q + m
                            lo_tiles(b_lo[:, kt], tiles(t2)[:, m], b_hi[:, kt], O_Z + kt + 1)
                if j == 2:
                    dve.wait_ge(s_ab_hi, 1)
                    nc.vector.tensor_tensor(ab_lo[:], ab_raw[:], ab_hi[:].bitcast(F32), ALU.subtract
                                            ).then_inc(own.up(s_ab_lo), 1)
                lo_parts(slab_of(Num(G_WOUT + j)) + AHEAD, SLABS)

            dve.wait_ge(s_ab_mm, 1)
            nc.vector.tensor_copy(ab_c[0:2 * HEADS], misc[0:2 * HEADS, 1536:1536 + T]
                ).then_inc(own.up(s_ab_dve), 1)
            dve.wait_ge(s_ab_mm, 2)
            ab = misc[:, 1536:1600].rearrange("p (a h) -> p a h", a=2)
            halves = [ab_t[:, k].rearrange("p (a h) -> p a h", a=2) for k in range(5)]
            dtb = vecs[:, V_DTB:V_DTB + HEADS].unsqueeze(1).to_broadcast([P, 2, HEADS])
            add(halves[0], ab[:, :, 0:HEADS], dtb, done=s_ab_dve)
            dve.wait_ge(*own.last())
            nc.vector.tensor_scalar(ab_t[:, 1], ab_t[:, 0], -1.0, None, ALU.mult).then_inc(own.up(s_ab_dve), 1)
            dve.wait_ge(*own.last())
            add(ab_t[:, 1], ab_t[:, 0], ab_t[:, 1], ALU.min, done=s_ab_dve)
            nc.vector.tensor_scalar(ab_t[:, 0], ab_t[:, 0], 0.0, None, ALU.max).then_inc(own.up(s_dve), 1)
            dve.wait_ge(s_ab_act, 2)
            nc.vector.tensor_scalar(ab_t[:, 3], ab_t[:, 3], 1.0, None, ALU.add).then_inc(own.up(s_dve), 1)
            dve.wait_ge(*own.last())
            nc.vector.reciprocal(beta[:], ab_t[:, 3]).then_inc(own.up(s_dve), 1)
            dve.wait_ge(s_ab_act, 4)
            add(ab_t[:, 0], ab_t[:, 0], ab_t[:, 2], done=s_ab_dve)
            dve.wait_ge(*own.last())
            nc.vector.scalar_tensor_tensor(
                out=decay[:].rearrange("p (a h) -> p a h", a=2), in0=halves[0], scalar=-1.0,
                in1=ab_t[:, 4, 0:HEADS].unsqueeze(1).to_broadcast([P, 2, HEADS]), op0=ALU.mult, op1=ALU.mult
                    ).then_inc(own.up(s_ab_dve), 1)

            def other_taps(g, par, to):
                col = (g + (-G_A)).times(16) + V_CONV
                dve.wait_ge(*own.last())
                nc.vector.tensor_copy(conv_now[:], vecs[:, bass.ds(col.v, 16)]).then_inc(own.up(s_dve), 1)
                dve.wait_ge(*own.last())
                dve.wait_ge(s_tap, (g + (1 - G_A)).times(4).v)
                for d in range(1, 4):
                    for m in range(GM):
                        if d > 1:
                            dve.wait_ge(*own.last(GM))
                        out = tiles(to)[:, m, d:T]
                        src = acc[:, par, m * T:(m + 1) * T - d]
                        ins = nc.vector.scalar_tensor_tensor(out=out, in0=src,
                                                             scalar=conv_now[:, 4 * m + 3 - d:4 * m + 4 - d],
                                                             in1=out, op0=ALU.mult, op1=ALU.add)
                        ins.then_inc(own.up(s_free if (d, m) == (3, GM - 1) else s_dve), 1)

            def pair_products(out, done):
                for h in range(BATCH):
                    for half, k, w in ((0, h * T, T), (1, BATCH * T + h * P, P)):
                        last = (h, half) == (BATCH - 1, 1)
                        scaled(out[:, k:k + w], misc[:, k:k + w], beta_now[:, half, h:h + 1], dec_t[:, k:k + w],
                               done=done if last else None)

            with dve.Fori(0, 4) as i:
                own.enter(i, {s_dve: 39, s_free: 2, s_qkn: 2, s_l: 1, s_a: 1, s_lo: 16})
                for k, out in ((0, q_n), (1, k_n)):
                    g = Num(G_A + k, i, 2)
                    n = slab_of(g) + AHEAD
                    other_taps(g, k, t0)
                    lo_parts(n, 5)
                    dve.wait_ge(s_rinv, Num(1 + k, i, 2).v)
                    add(out[:], t1[:, 0:4 * T], t3[:], ALU.mult, done=s_qkn)
                    lo_parts(n + 5, 1)
                    if k:
                        nc.vector.tensor_copy(
                            beta_now[:], beta[:].rearrange("p (a h) -> p a h", a=2)[:, :, bass.ds(i * BATCH, BATCH)]
                                ).then_inc(own.up(s_dve), 1)
                        dve.wait_ge(*own.last())
                        dve.wait_ge(s_em, Num(2, i, 2).v)
                        dve.wait_ge(s_kk, Num(1, i, 1).v)
                        pair_products(l_t, s_l)
                    lo_parts(n + 6, 1)
                    if k:
                        dve.wait_ge(s_qk, Num(1, i, 1).v)
                        pair_products(a_t, s_a)
                    lo_parts(n + 7, 1)
                own.leave(4)

            def invert(s):
                below = 31 - s
                tmp = prod[:, 0:below * (s + 1)].rearrange("p (t c) -> p t c", t=below)
                row = inv[:, s, 0:s + 1].unsqueeze(1).to_broadcast([P, below, s + 1])
                col = blk[:, s, s + 1:32].unsqueeze(2).to_broadcast([P, below, s + 1])
                dve.wait_ge(*own.last())
                add(tmp, col, row, ALU.mult)
                dve.wait_ge(*own.last())
                add(inv[:, s + 1:32, 0:s + 1], inv[:, s + 1:32, 0:s + 1], tmp, ALU.subtract)

            def solve_updates(j, step):
                if step in (1, 3):
                    dve.wait_ge(s_solve_pe, 8 * j + step + 1)
                    y = t0[:, 0:1024]
                    add(y, y, misc[:, 1024:2048], ALU.subtract, done=s_solve_dve if step == 3 else None)
                    if step == 1:
                        x = t1[:, 0:1024]
                        add(x, x, misc[:, 0:1024], ALU.subtract, done=s_solve_dve)
                if step == 5:
                    dve.wait_ge(s_solve_pe, 8 * j + 6)
                    v = vo[:, BATCH * j:BATCH * (j + 1), P:T]
                    add(v, v, misc[:, 512:1024].rearrange("p (h t) -> p h t", h=BATCH), ALU.subtract,
                        done=s_solve_dve)

            rows = {G_A + 8: (1, range(0, 13)), G_A + 9: (0, range(13, 31))}
            for g in range(G_A + 8, G_AOUT):
                n = slab_of(Num(g)) + AHEAD
                j = g - G_A - 12
                dve.wait_ge(*own.last())
                if j < 0:
                    other_taps(Num(g), g % 2, t4)
                for k in range(8):
                    if g >= G_A + 11 and g < G_AOUT - 1 and k:
                        solve_updates(j + 1, k - 1)
                    if g in rows:
                        k0, which = rows[g]
                        if g == G_A + 8 and k == k0:
                            nc.vector.memset(inv[:], 0.0).then_inc(own.up(s_dve), 1)
                            dve.wait_ge(*own.last())
                            flat = inv[:].rearrange("p a b -> p (a b)")
                            nc.vector.memset(flat[:, 0:1024:33], 1.0).then_inc(own.up(s_dve), 1)
                            dve.wait_ge(s_blk, 16 * 8)
                        if k >= k0:
                            part = -(-len(which) // (8 - k0))
                            for r in which[(k - k0) * part:(k - k0 + 1) * part]:
                                invert(r)
                        if g == G_A + 9 and k == 7:
                            dve.wait_ge(*own.last())
                            nc.vector.tensor_copy(inv_t[:], inv[:].rearrange("p t s -> p s t")
                                ).then_inc(own.up(s_inv), 1)
                    last = g == G_AOUT - 1
                    o = wide(vo, 4 * j) if j >= 0 else None
                    if j >= 0 and k == (1 if last else 5):
                        dve.wait_ge(s_rinv, 9 + j)
                        scaled(o, o, vecs[:, V_ONW:V_ONW + 1], t4[:], done=s_on)
                    if j >= 0 and k == (2 if last else 6):
                        dve.wait_ge(*own.last())
                        dve.wait_ge(s_zs, j + 1)
                        add(o, o, t4[:], ALU.mult, done=s_tmp)
                        dve.sem_inc(own.also(s_free), 1)
                    if j >= 0 and k == (3 if last else 7):
                        lo_tiles(wide(a_lo, 4 * j), o, wide(a_hi, 4 * j), O_A + 1 + j)
                    lo_parts(n + k, 1)

            dve.wait_ge(s_xb, 16)
            for j in range(4):
                dve.wait_ge(s_used, slab_of(Num(G_AOUT + j + 1)).c)
                add(wide(xres, 4 * j), acc[:, j % 2], wide(xres, 4 * j), done=s_x1)
                dve.sem_inc(own.also(s_free), 1)
                if j in (1, 2):
                    dve.wait_ge(s_sq, 24 + j + 1)
                    add(t3[:], t3[:], t0[:, 0:4 * T], done=s_sums)
                if j == 3:
                    dve.wait_ge(s_root, 4)
                    for q in range(4):
                        dve.wait_ge(*own.last())
                        for m in range(GM):
                            kt = 4 * q + m
                            scaled(tiles(t2)[:, m], xres[:, kt], vecs[:, V_NW1 + kt:V_NW1 + kt + 1], r1[:], s_tmp)
                        for m in range(GM):
                            kt = 4 * q + m
                            lo_tiles(b_lo[:, kt], tiles(t2)[:, m], b_hi[:, kt], O_AO + kt + 1)
                lo_parts(slab_of(Num(G_AOUT + j)) + AHEAD, SLABS)

            def by_head(t, k, w):
                return t[:, k:k + BATCH * w].rearrange("p (h s) -> p h s", h=BATCH)

            with dve.Fori(0, 4) as i:
                own.enter(i, {s_free: 4, s_sql: 2, s_bn: 2, s_biased: 1, s_max: 1, s_pn: 1, s_ptc_dve: 1, s_tmp: 1,
                              s_opnd: 1, s_dve: 6, s_lo: 32})
                for k, (out, w) in enumerate(((t2, V_QNW), (t0, V_KNW))):
                    n = slab_of(Num(G_B + k, i, 4)) + AHEAD
                    dve.wait_ge(s_sq2, Num(13 + k, i, 2).v)
                    dve.sem_inc(own.also(s_free), 1)
                    dve.wait_ge(s_sqh, Num(1 + k, i, 2).v)
                    nc.vector.tensor_tensor(sq_lo[:], t1[:, 0:4 * T], sq_hi[:].bitcast(F32), ALU.subtract
                                            ).then_inc(own.up(s_sql), 1)
                    lo_parts(n, 5)
                    dve.wait_ge(s_rinv, Num(13 + k, i, 2).v)
                    scaled(out[:, 0:4 * T], t0[:, 0:4 * T], vecs[:, w:w + 1], t3[:], done=s_bn)
                    lo_parts(n + 5, 2)
                    if k:
                        dve.wait_ge(s_score, Num(1, i, 1).v)
                        dve.wait_ge(s_bias, Num(16, i, 16).v)
                        for half, at_, w in halves_of_pairs():
                            add(by_head(p_t, at_, w), by_head(misc, at_, w), by_head(t4, 0, T)[:, :, T - w:T],
                                done=None if half else s_biased)
                        dve.wait_ge(*own.last())
                        for half, at_, w in halves_of_pairs():
                            nc.vector.memset(by_head(p_t, at_, w)[0:CHUNK, :, w - CHUNK:w], MASKED
                                ).then_inc(own.up(s_dve), 1)
                        dve.wait_ge(*own.last())
                        for half, at_, w in halves_of_pairs():
                            nc.vector.tensor_reduce(row_max[:, half], by_head(p_t, at_, w),
                                                            mybir.AxisListType.X, ALU.max, negate=True
                                                                ).then_inc(own.up(s_dve if half else s_max), 1)
                    lo_parts(n + 7, 1)
                n = slab_of(Num(G_B + 2, i, 4)) + AHEAD
                dve.wait_ge(s_vn, Num(1, i, 1).v)
                dve.sem_inc(own.also(s_free), 1)
                lo_parts(n, 3)
                dve.wait_ge(s_prob, Num(1, i, 1).v)
                nc.vector.reciprocal(row_sum[:], row_sum[:]).then_inc(own.up(s_dve), 1)
                dve.wait_ge(*own.last())
                for half, at_, w in halves_of_pairs():
                    p = by_head(p_t, at_, w)
                    add(p, p, row_sum[:, half].unsqueeze(2).to_broadcast([P, BATCH, w]), ALU.mult,
                        done=None if half else s_pn)
                lo_parts(n + 3, 3)
                dve.wait_ge(s_pt, Num(1, i, 1).v)
                nc.vector.tensor_copy(p_tt[:, BATCH * T:PAIRS], misc[:, BATCH * T:PAIRS]
                    ).then_inc(own.up(s_ptc_dve), 1)
                lo_parts(n + 6, 2)
                n = n + SLABS
                dve.wait_ge(s_zb, Num(1, i, 1).v)
                dve.wait_ge(s_pv, Num(1, i, 1).v)
                add(t1[:, 0:4 * T], t1[:, 0:4 * T], misc[:, 0:4 * T], ALU.mult, done=s_tmp)
                dve.sem_inc(own.also(s_free), 1)
                lo_parts(n, 2)
                dve.wait_ge(s_rnd, Num(O_B + 1, i, 1).v)
                nc.vector.tensor_tensor(
                    a_lo[:, bass.ds(i * 4, 4)].rearrange("p k t -> p (k t)"), t1[:, 0:4 * T],
                    a_hi[:, bass.ds(i * 4, 4)].rearrange("p k t -> p (k t)").bitcast(F32), ALU.subtract
                        ).then_inc(own.up(s_opnd), 1)
                lo_parts(n + 2, 6)
                own.leave(4)
            for j in range(4):
                dve.wait_ge(s_used, slab_of(Num(G_BOUT + j + 1)).c)
                add(wide(vo, 4 * j), acc[:, j % 2], wide(xres, 4 * j), done=s_y)
                dve.sem_inc(own.also(s_free), 1)
                lo_parts(slab_of(Num(G_BOUT + j)) + AHEAD, SLABS)



def slabs(m, groups):
    k = m.shape[0]
    cols = np.stack([m[:, c:c + GC] for c in groups])
    s = cols.reshape(len(groups), k // (SLAB_K * P), SLAB_K, P, GC).transpose(0, 1, 3, 2, 4)
    return s.reshape(-1, P, SLAB_K * GC)


def channels(v):
    return v.reshape(-1, P).T


def build_stream(i):
    w_in = i["pool_w_in"][0]
    ug = slabs(w_in, [c for j in range(4) for c in (GC * j, D + GC * j)])
    gate = i["w_mod"][0][:, 2 * D:].reshape(KT, P, 2, D // 2).transpose(0, 2, 1, 3).reshape(GATES, 1, P, D // 2)
    ug = np.concatenate([ug.reshape(GATES, 2, P, SLAB_K * GC), gate], axis=1).reshape(-1, P, SLAB_K * GC)
    grp = np.concatenate([slabs(i["pool_w_grp"][0, j], [0]) for j in range(4)])
    quarters = [GC * j for j in range(4)]
    a = i["a_w_in_2"][0]
    order_a = [c for j in range(4) for c in (GC * j, D + GC * j)]
    order_a += [2 * D + GC * j for j in range(4)] + [3 * D + GC * j for j in range(4)]
    order_b = [k * D + GC * j for j in range(4) for k in range(4)]
    return np.concatenate([ug, grp, slabs(i["pool_w_out"][0], quarters), slabs(a, order_a),
                           slabs(i["a_w_out_2"][0], quarters), slabs(i["b_w_in_2"][0], order_b),
                           slabs(i["b_w_out_2"][0], quarters)]).reshape(-1, SLAB_K * GC), order_a


def build_vecs(i, order_a):
    conv = i["a_conv_w_2"][0]
    conv = np.stack([conv[:, c + P * m:c + P * (m + 1)] for c in order_a[:12] for m in range(GM)])
    edges = np.zeros((4, 2 * PAD), np.float32)
    for j, w in enumerate(WINDOWS):
        for k, t in enumerate([*range(PAD), *range(T - PAD, T)]):
            edges[j, k] = 1.0 / (min(t + w // 2, T) - max(t - w // 2, 0))
    rows = [i["a_a_log_2"][0], i["a_dt_bias_2"][0], edges.reshape(-1)]
    return np.concatenate([
        channels(i["c"][0]), channels(i["b_mod"][0]), channels(i["pool_scale"][0]), channels(i["final_norm_g"]),
        channels(i["norm_w_2"][0]), channels(i["norm_w_2"][1]), conv.transpose(2, 0, 1).reshape(P, -1),
        i["a_out_norm_w_2"].T, i["b_q_norm_w_2"].T, i["b_k_norm_w_2"].T,
        *[np.broadcast_to(r, (P, r.size)) for r in rows]], axis=1)


def build_consts():
    r, c = np.arange(P)[:, None], np.arange(P)[None, :]
    one = np.ones((P, P))
    half, quarter = c // 64 == r // 64, c // 32 == r // 32
    return np.concatenate([r == c, r > c, one, r <= c, one, quarter, half & ~quarter, ~half],
                          axis=1).astype(np.float32)


def kernel(**inputs):
    import concourse.bacc as bacc
    from concourse.bass_utils import run_bass_kernel_spmd

    i = {k: np.asarray(v) for k, v in inputs.items()}
    stream, order_a = build_stream(i)
    mod = i["w_mod"][0][:, :2 * D].reshape(KT, P, 2, D).transpose(2, 0, 1, 3).reshape(2 * KT, P, D)
    rel = i["b_rel_bias_2"][0]
    arrays = {
        "weights": stream,
        "mod_w": mod,
        "x_t": i["x"][0].T.reshape(KT, P, T).transpose(1, 0, 2),
        "vecs": build_vecs(i, order_a),
        "consts": build_consts(),
        "w_ab": i["a_w_in_2"][0][:, 4 * D:].reshape(KT, P, 2 * HEADS).transpose(1, 0, 2),
        "bias": rel[:, ::-1],
    }
    arrays = {k: np.ascontiguousarray(v) for k, v in arrays.items()}
    nc = bacc.Bacc("TRN2", target_bir_lowering=False, num_devices=1)
    args = [nc.dram_tensor(k, v.shape, F32, kind="ExternalInput").ap() for k, v in arrays.items()]
    out = nc.dram_tensor("out", (P, KT, T), F32, kind="ExternalOutput").ap()
    program(nc, *args, out)
    r = run_bass_kernel_spmd(nc, [arrays], core_ids=[0])
    return r.results[0]["out"].transpose(2, 1, 0).reshape(1, T, D)
```
